# Optimizing a Trainium2 kernel written in Bass

```python
import math
import jax, jax.numpy as jnp
from jax import lax
import numpy as np

D_MODEL = 1024
BATCH = 1
SEQ = 128
DEPTH = 2
DEC_BATCH = 1
DEC_SEQ = 512
PAST_LEN = 128

GRID_W = 64
N_HEADS = 16
N_KV_HEADS = 4
HEAD_DIM = D_MODEL // N_HEADS
AXIS_DIM = HEAD_DIM // 2
ROPE_THETA = 10000.0
Q_BLOCK = 128
N_ATTN_LAYERS = (DEPTH + 1) // 2
N_CONV_LAYERS = DEPTH // 2
CONV_W = 3
PEER_HEADS = 8
N_KEYS = 128
N_EXPERTS = N_KEYS * N_KEYS
D_KEY = 256
D_KEY_HALF = D_KEY // 2
PEER_TOPK = 16
TOK_BLOCK = 128
N_MOD = 6
EPS = 1e-6

kernel_name = "hybrid_dit_gqa_shortconv_peer_step"

def rmsnorm(x, g):
    xf = x.astype(jnp.float32)
    y = xf * lax.rsqrt(jnp.mean(xf * xf, axis=-1, keepdims=True) + EPS)
    return (y * g.astype(jnp.float32)).astype(x.dtype)

def modulation(cond, w_ada, b_ada):
    m = jax.nn.silu(cond) @ w_ada + b_ada
    return [t[:, None, :] for t in jnp.split(m, N_MOD, axis=-1)]

def modulate(h, shift, scale):
    return h * (1 + scale) + shift

def axial_angles(n_tokens):
    n_rows = n_tokens // GRID_W
    row = jnp.repeat(jnp.arange(n_rows, dtype=jnp.float32), GRID_W)
    col = jnp.tile(jnp.arange(GRID_W, dtype=jnp.float32), n_rows)
    inv = ROPE_THETA ** (-jnp.arange(0, AXIS_DIM, 2, dtype=jnp.float32) / AXIS_DIM)
    return row[:, None] * inv, col[:, None] * inv

def rope_axis(xa, ang):
    cos = jnp.cos(ang)[:, None, :].astype(xa.dtype)
    sin = jnp.sin(ang)[:, None, :].astype(xa.dtype)
    x1, x2 = jnp.split(xa, 2, axis=-1)
    return jnp.concatenate([x1 * cos - x2 * sin, x2 * cos + x1 * sin], axis=-1)

def axial_rope(x, ang_row, ang_col):
    return jnp.concatenate([rope_axis(x[..., :AXIS_DIM], ang_row),
                            rope_axis(x[..., AXIS_DIM:], ang_col)], axis=-1)

def qkv_project(h, w_qkv, q_gain, k_gain):
    B, S, _ = h.shape
    qkv = h @ w_qkv
    q, k, v = jnp.split(qkv, [N_HEADS * HEAD_DIM, (N_HEADS + N_KV_HEADS) * HEAD_DIM], axis=-1)
    q = rmsnorm(q.reshape(B, S, N_HEADS, HEAD_DIM), q_gain)
    k = rmsnorm(k.reshape(B, S, N_KV_HEADS, HEAD_DIM), k_gain)
    v = v.reshape(B, S, N_KV_HEADS, HEAD_DIM)
    return q, k, v

def blocked_attention(q, k, v):
    B, S, H, Dh = q.shape
    G = H // N_KV_HEADS
    qb = q.reshape(B, S // Q_BLOCK, Q_BLOCK, N_KV_HEADS, G, Dh).transpose(1, 0, 2, 3, 4, 5)
    scale = Dh ** -0.5

    def one_block(qblk):
        s = jnp.einsum('bqhgd,bkhd->bhgqk', qblk, k).astype(jnp.float32) * scale
        p = jax.nn.softmax(s, axis=-1).astype(v.dtype)
        return jnp.einsum('bhgqk,bkhd->bqhgd', p, v)

    out = lax.map(one_block, qb)
    return out.transpose(1, 0, 2, 3, 4, 5).reshape(B, S, H * Dh)

def short_conv_mixer(h, w_bcx, conv_w, conv_b, w_out):
    gb, gc, xin = jnp.split(h @ w_bcx, 3, axis=-1)
    u = gc * xin
    up = jnp.pad(u, ((0, 0), (1, 1), (0, 0)))
    S = u.shape[1]
    conv = (up[:, 0:S] * conv_w[0] + up[:, 1:S + 1] * conv_w[1]
            + up[:, 2:S + 2] * conv_w[2] + conv_b)
    return (gb * conv) @ w_out

def peer(h, w_pq, sub_keys, u_exp, v_exp):
    B, S, D = h.shape
    hb = h.reshape((B * S) // TOK_BLOCK, TOK_BLOCK, D)

    def one_block(xb):
        q = (xb @ w_pq).reshape(TOK_BLOCK, PEER_HEADS, 2, D_KEY_HALF)
        s = jnp.einsum('thcd,hcnd->thcn', q, sub_keys).astype(jnp.float32)
        s1, i1 = lax.top_k(s[:, :, 0], PEER_TOPK)
        s2, i2 = lax.top_k(s[:, :, 1], PEER_TOPK)
        cand_s = (s1[..., :, None] + s2[..., None, :]).reshape(TOK_BLOCK, PEER_HEADS, PEER_TOPK * PEER_TOPK)
        cand_i = (i1[..., :, None] * N_KEYS + i2[..., None, :]).reshape(TOK_BLOCK, PEER_HEADS, PEER_TOPK * PEER_TOPK)
        top_s, pos = lax.top_k(cand_s, PEER_TOPK)
        eidx = jnp.take_along_axis(cand_i, pos, axis=-1)
        g = jax.nn.softmax(top_s, axis=-1)
        u = jnp.take(u_exp, eidx, axis=0)
        a = jax.nn.gelu(jnp.einsum('thkd,td->thk', u, xb).astype(jnp.float32))
        w = (g * a).astype(xb.dtype)
        return jnp.einsum('thk,thkd->td', w, jnp.take(v_exp, eidx, axis=0))

    return lax.map(one_block, hb).reshape(B, S, D)

def setup_inputs(seed: int = 0) -> dict:
    key = jax.random.key(seed)
    ks = jax.random.split(key, 24)
    f32 = jnp.float32
    D = D_MODEL
    nrm = lambda k, shape, s: jax.random.normal(k, shape, f32) * s
    qkv_cols = (N_HEADS + 2 * N_KV_HEADS) * HEAD_DIM
    return {
        "x_prompt": nrm(ks[0], (BATCH, SEQ, D), 1.0),
        "x_sample": nrm(ks[1], (DEC_BATCH, DEC_SEQ, D), 1.0),
        "cache_k": nrm(ks[2], (DEC_BATCH, N_ATTN_LAYERS, PAST_LEN, N_KV_HEADS, HEAD_DIM), 1.0),
        "cache_v": nrm(ks[3], (DEC_BATCH, N_ATTN_LAYERS, PAST_LEN, N_KV_HEADS, HEAD_DIM), 1.0),
        "c": nrm(ks[4], (DEC_BATCH, D), 1.0),
        "c_ctx": nrm(ks[5], (D,), 1.0),
        "w_ada": nrm(ks[6], (DEPTH, D, N_MOD * D), 0.5 * D ** -0.5),
        "b_ada": nrm(ks[7], (DEPTH, N_MOD * D), 0.02),
        "norm_mix": 1.0 + nrm(ks[8], (DEPTH, D), 0.02),
        "norm_ffn": 1.0 + nrm(ks[9], (DEPTH, D), 0.02),
        "norm_final": 1.0 + nrm(ks[10], (D,), 0.02),
        "w_qkv": nrm(ks[11], (N_ATTN_LAYERS, D, qkv_cols), D ** -0.5),
        "q_gain": 1.0 + nrm(ks[12], (N_ATTN_LAYERS, HEAD_DIM), 0.02),
        "k_gain": 1.0 + nrm(ks[13], (N_ATTN_LAYERS, HEAD_DIM), 0.02),
        "w_o": nrm(ks[14], (N_ATTN_LAYERS, N_HEADS * HEAD_DIM, D), (N_HEADS * HEAD_DIM) ** -0.5),
        "w_bcx": nrm(ks[15], (N_CONV_LAYERS, D, 3 * D), D ** -0.5),
        "conv_w": nrm(ks[16], (N_CONV_LAYERS, CONV_W, D), CONV_W ** -0.5),
        "conv_b": nrm(ks[17], (N_CONV_LAYERS, D), 0.02),
        "w_conv_out": nrm(ks[18], (N_CONV_LAYERS, D, D), D ** -0.5),
        "w_pq": nrm(ks[19], (DEPTH, D, PEER_HEADS * D_KEY), D ** -0.5),
        "sub_keys": nrm(ks[20], (DEPTH, PEER_HEADS, 2, N_KEYS, D_KEY_HALF), D_KEY_HALF ** -0.5),
        "u_exp": nrm(ks[21], (DEPTH, N_EXPERTS, D), D ** -0.5),
        "v_exp": nrm(ks[22], (DEPTH, N_EXPERTS, D), PEER_HEADS ** -0.5),
    }

def reference(x_prompt, x_sample, cache_k, cache_v, c, c_ctx, w_ada, b_ada,
              norm_mix, norm_ffn, norm_final, w_qkv, q_gain, k_gain, w_o,
              w_bcx, conv_w, conv_b, w_conv_out, w_pq, sub_keys, u_exp, v_exp):
    xp = x_prompt
    xs = x_sample
    ang_row, ang_col = axial_angles(xs.shape[1])
    new_k, new_v = [], []
    for i in range(DEPTH):
        j = i // 2
        sh_m_c, sc_m_c, g_m_c, sh_f_c, sc_f_c, g_f_c = modulation(c_ctx[None, :], w_ada[i], b_ada[i])
        sh_m_s, sc_m_s, g_m_s, sh_f_s, sc_f_s, g_f_s = modulation(c, w_ada[i], b_ada[i])
        hp = modulate(rmsnorm(xp, norm_mix[i]), sh_m_c, sc_m_c)
        hs = modulate(rmsnorm(xs, norm_mix[i]), sh_m_s, sc_m_s)
        if i % 2 == 0:
            qc, kc, vc = qkv_project(hp, w_qkv[j], q_gain[j], k_gain[j])
            new_k.append(kc)
            new_v.append(vc)
            mp = blocked_attention(qc, kc, vc) @ w_o[j]
            qs, ks_, vs = qkv_project(hs, w_qkv[j], q_gain[j], k_gain[j])
            qs = axial_rope(qs, ang_row, ang_col)
            ks_ = axial_rope(ks_, ang_row, ang_col)
            k_all = jnp.concatenate([ks_, cache_k[:, j]], axis=1)
            v_all = jnp.concatenate([vs, cache_v[:, j]], axis=1)
            ms = blocked_attention(qs, k_all, v_all) @ w_o[j]
        else:
            mp = short_conv_mixer(hp, w_bcx[j], conv_w[j], conv_b[j], w_conv_out[j])
            ms = short_conv_mixer(hs, w_bcx[j], conv_w[j], conv_b[j], w_conv_out[j])
        xp = xp + g_m_c * mp
        xs = xs + g_m_s * ms
        hp = modulate(rmsnorm(xp, norm_ffn[i]), sh_f_c, sc_f_c)
        hs = modulate(rmsnorm(xs, norm_ffn[i]), sh_f_s, sc_f_s)
        xp = xp + g_f_c * peer(hp, w_pq[i], sub_keys[i], u_exp[i], v_exp[i])
        xs = xs + g_f_s * peer(hs, w_pq[i], sub_keys[i], u_exp[i], v_exp[i])
    y_prompt = rmsnorm(xp, norm_final)
    y_sample = rmsnorm(xs, norm_final)
    new_cache_k = jnp.stack(new_k, axis=1)
    new_cache_v = jnp.stack(new_v, axis=1)
    return (y_prompt, y_sample, new_cache_k, new_cache_v)


_drawn_inputs = setup_inputs


def setup_inputs(seed=0):
    import zlib

    import numpy as np

    out = dict(_drawn_inputs(seed))
    spreads = {}
    factors = {'cache_k': 5.233,
     'cache_v': 4.45,
     'norm_mix': 2.99,
     'norm_ffn': 4.348,
     'norm_final': 8.329,
     'q_gain': 8.0,
     'k_gain': 2.833,
     'conv_b': 27.588}
    for name, (base, spread) in spreads.items():
        noise = np.random.default_rng([zlib.crc32(name.encode()), seed]).standard_normal(out[name].shape)
        drawn = base * np.exp(spread * noise) if base else spread * noise
        out[name] = __import__('jax').numpy.asarray(drawn.astype(out[name].dtype))
    for name, factor in factors.items():
        out[name] = (out[name] * factor).astype(out[name].dtype)
    return out
```

```python
import math

import numpy as np

import concourse.bass as bass
from concourse import mybir

P = 128
ALU = mybir.AluOpType
ACT = mybir.ActivationFunctionType
F32 = mybir.dt.float32
F32R = mybir.dt.float32r
U32 = mybir.dt.uint32
AX_X = mybir.AxisListType.X

D = 1024
DJ = D // P
NS = 512
NP = 128
NT = NS + NP
TT = NT // P
DEPTH = 2
HEADS, KVH, HD = 16, 4, 64
GRID_W = 64
PH, NKEY, TOPK = 8, 128, 16
HC = PH * 2
PICKS = PH * TOPK
EPS = 1e-6
LOWEST = -3.0e38

RAW = 4
N_ADA, N_QKV, N_WO, N_PQ, N_BCX, N_CO = 48, 12, 8, 16, 24, 8
STREAM = [("ada", N_ADA), ("qkv", N_QKV), ("wo", N_WO), ("pq", N_PQ),
          ("ada1", N_ADA), ("bcx", N_BCX), ("co", N_CO), ("pq1", N_PQ)]
RAW_AT, SPLIT_AT = {}, {}
_r = _s = 0
for _name, _n in STREAM:
    RAW_AT[_name], SPLIT_AT[_name] = _r, _s
    _r += _n
    if not _name.startswith("ada"):
        _s += _n
N_RAW, N_SPLIT = _r, _s
RING = 8

C_MEAN, C_HEAD, C_SWAP, C_ID, C_J16, C_COS, C_SIN = 0, 128, 256, 384, 512, 528, 1040
C_ALL = 1552


def hybrid_step(nc, xT, cond, consts, wstream, bada, gains, hgain, convp, kcache, vcache, subk,
                u_exp, v_exp, yT, k_new, v_new):
    off = [16512]

    def sb(name, shape, dt, at=None):
        size = int(np.prod(shape[1:])) * 4
        if at is None:
            at = off[0]
            off[0] += size
        return nc.alloc_sbuf_tensor_at(name, shape, dt, offset=at), at

    X, _ = sb("X", [P, DJ, NT], F32)
    H, at_H = sb("H", [P, DJ, NT], F32)
    HH, at_HH = sb("HH", [P, DJ, NT], F32R)
    HL, _ = sb("HL", [P, DJ, NT], F32R)
    BIG, _ = sb("BIG", [P, HC, NT], F32)
    RW, _ = sb("RW", [P, RAW, DJ, P], F32)
    SH, _ = sb("SH", [P, 2, DJ, P], F32R)
    SL, _ = sb("SL", [P, 2, DJ, P], F32R)
    SK, _ = sb("SK", [P, HC, NKEY], F32)
    CO, _ = sb("CO", [P, C_ALL], F32)
    CAND, at_CAND = sb("CAND", [P, PH, TOPK, TOPK], F32)
    WK, at_WK = sb("WK", [P, HC, NKEY], F32)
    HTOK, _ = sb("HTOK", [P, D], F32)
    ACC, _ = sb("ACC", [P, D], F32)
    small, _ = sb("small", [P, 1024], F32)
    at_small = [off[0] - 4096]

    def tiny(name, n, dt=F32, shape=None):
        t, _ = sb(name, shape or [P, n], dt, at=at_small[0])
        at_small[0] += 32 * -(-n // 8)
        return t

    CS = tiny("CS", 16, shape=[P, DJ, 2])
    M = tiny("M", 96, shape=[P, N_ADA, 2])
    GS = tiny("GS", 32, shape=[P, 2, DJ, 2])
    BA = tiny("BA", 96, shape=[P, DEPTH, N_ADA])
    GN = tiny("GN", 40, shape=[P, 5, DJ])
    HG = tiny("HG", 10)
    CV = tiny("CV", 32, shape=[P, DJ, 4])
    EP = tiny("EP", 1)
    MX = tiny("MX", 2)
    NB = tiny("NB", 2)
    RS = tiny("RS", 2)
    RI = tiny("RI", 2)
    A16 = tiny("A16", 16)
    Z = tiny("Z", 8)
    assert at_small[0] <= off[0]
    V16, _ = sb("V16", [P, HC, TOPK], F32)
    I16, _ = sb("I16", [P, HC, TOPK], U32)
    IF, _ = sb("IF", [P, HC, TOPK], F32)
    TS, _ = sb("TS", [P, PH, TOPK], F32)
    PO, _ = sb("PO", [P, PH, TOPK], U32)
    AB, _ = sb("AB", [P, 2, PICKS], U32)
    ABF, _ = sb("ABF", [P, 2, PICKS], F32)
    I12, _ = sb("I12", [P, 2, PICKS], F32)
    EI, _ = sb("EI", [P, PICKS], U32)
    EIS, _ = sb("EIS", [P, 2, 8], U32)
    G, _ = sb("G", [P, PH, TOPK], F32)
    AA, _ = sb("AA", [P, PICKS], F32)
    WW, _ = sb("WW", [P, PICKS], F32)
    ROWS, _ = sb("ROWS", [P, RING, D], F32, at=at_HH)
    EQ, _ = sb("EQ", [P, PICKS, TOPK], F32, at=at_WK)
    SQ, _ = sb("SQ", [P, 2, NT], F32, at=at_H)
    RN, _ = sb("RN", [P, 2, NT], F32, at=at_H + 2 * NT * 4)
    TR, _ = sb("TR", [P, 2, NS], F32, at=at_H + 4 * NT * 4)
    QS, _ = sb("QS", [P, NT], F32, at=at_H)
    PR, _ = sb("PR", [P, 2, NT], F32, at=at_H + NT * 4)
    PT, _ = sb("PT", [P, 2, NT], F32, at=at_H + 3 * NT * 4)
    KC, _ = sb("KC", [P, 2, P], F32, at=at_CAND)
    VC, _ = sb("VC", [P, 2 * P], F32, at=at_CAND + 1024)
    GC, _ = sb("GC", [P, NT], F32, at=at_WK)
    UU, _ = sb("UU", [P, NT], F32, at=at_WK + 2560)
    CC, _ = sb("CC", [P, NT], F32, at=at_CAND)
    RR, _ = sb("RR", [P, NT], F32, at=at_CAND + 2560)

    PS = nc.alloc_psum_tensor("PS", [P, 8, 512], F32)
    PSf = PS[:].rearrange("p b n -> p (b n)")

    def ps_pair(par):
        return PSf[:, par * 1024:par * 1024 + NT]

    MEAN, HEADM, SWAP, ID = (CO[:, c:c + P] for c in (C_MEAN, C_HEAD, C_SWAP, C_ID))
    J16 = CO[:, C_J16:C_J16 + 16]
    COS, SIN = CO[:, C_COS:C_COS + NS], CO[:, C_SIN:C_SIN + NS]

    sem = nc.alloc_semaphore
    x_in, small_in, const_in, cache_in = sem("x_in"), sem("small_in"), sem("const_in"), sem("cache_in")
    sk_in = sem("sk_in")
    raw_in = [sem(f"raw_in{k}") for k in range(RAW)]
    raw_used = sem("raw_used")
    hi_done = sem("hi_done")
    proj_done = sem("proj_done")
    evac_done = sem("evac_done")
    eps_done, cs_done, mod_done = sem("eps_done"), sem("cs_done"), sem("mod_done")
    sq_done, var_done, rt_done, xn_done = sem("sq_done"), sem("var_done"), sem("rt_done"), sem("xn_done")
    h_done, hl_done = sem("h_done"), sem("hl_done")
    hsq_done, hvar_done, hrt_done, hq_done, hrot_done, hrope_done = (
        sem(n) for n in ("hsq_done", "hvar_done", "hrt_done", "hq_done", "hrot_done", "hrope_done"))
    q_staged, score_done, nb_done, exp_done, p_done, pt_done, ptc_done, pv_done, o_done = (
        sem(n) for n in ("q_staged", "score_done", "nb_done", "exp_done", "p_done", "pt_done",
                         "ptc_done", "pv_done", "o_done"))
    oh_done = sem("oh_done")
    act_hi, act_lo = sem("act_hi"), sem("act_lo")
    route_ps, route_read = sem("route_ps"), sem("route_read")
    ht_ps, ht_done = sem("ht_ps"), sem("ht_done")
    sm_in, sm_out = sem("sm_in"), sem("sm_out")
    ei_done, stage_done = sem("ei_done"), sem("stage_done")
    row_in = [sem(f"row_in{k}") for k in range(RING)]
    rows_asked = sem("rows_asked")
    row_used = sem("row_used")
    a_done, g_done, acc_done, yt_done, peer_done = (
        sem(n) for n in ("a_done", "g_done", "acc_done", "yt_done", "peer_done"))
    y_done, out_done = sem("y_done"), sem("out_done")

    NORMS = [("mod", 0), ("peer", 0), ("mod", 1), ("peer", 1), ("final", 0)]

    def wait_x(eng, n):
        if n == 0:
            eng.wait_ge(x_in, 16)
        elif n in (1, 3):
            last = SPLIT_AT["pq"] if n == 1 else SPLIT_AT["pq1"]
            eng.wait_ge(evac_done, 2 + last)
        else:
            eng.wait_ge(peer_done, TT * (n // 2))

    block_cm = nc.Block()
    block = block_cm.__enter__()

    @block.sync
    def _(sp):
        sp.dma_start(CO[:], consts).then_inc(const_in, 16)
        sp.dma_start(CS[:], cond).then_inc(small_in, 16)
        sp.dma_start(BA[:], bada).then_inc(small_in, 16)
        sp.dma_start(GN[:], gains).then_inc(small_in, 16)
        sp.dma_start(HG[:], hgain).then_inc(small_in, 16)
        sp.dma_start(CV[:], convp).then_inc(small_in, 16)
        sp.dma_start(X[:], xT).then_inc(x_in, 16)

        def chunk(c, k):
            sp.dma_start(RW[:, k], wstream[bass.ds(c, 1)].rearrange("o p j n -> (o p) j n")).then_inc(raw_in[k], 16)

        for k in range(RAW):
            chunk(k, k)
        with sp.Fori(1, N_RAW // RAW) as g:
            for k in range(RAW):
                sp.wait_ge(raw_used, g * RAW + (k + 1 - RAW))
                chunk(g * RAW + k, k)

    @block.gpsimd
    def _(pool):
        def split_low(name, n):
            s0 = SPLIT_AT[name]
            with pool.Fori(0, n // RAW) as i:
                for k in range(RAW):
                    pool.wait_ge(hi_done, i * RAW + (s0 + k + 1))
                    nc.gpsimd.tensor_tensor(SL[:, k % 2], RW[:, k], SH[:, k % 2].bitcast(F32),
                                            ALU.subtract).then_inc(raw_used, 1)

        def gather(call, table):
            n0 = call * PICKS
            with pool.Fori(0, PICKS // 16) as i:
                for par in range(2):
                    nc.gpsimd.tensor_copy(EIS[:, par], EI[:, bass.ds(i * 16 + par * 8, 8)]).then_inc(stage_done, 1)
                    pool.wait_ge(stage_done, i * 2 + (call * 16 + par + 1))
                    for k in range(8):
                        pool.wait_ge(row_used, i * 16 + (n0 + par * 8 + k + 1))
                        pool.sem_inc(rows_asked)
                        nc.gpsimd.indirect_dma_start(
                            ROWS[:, k], None, table,
                            bass.IndirectOffsetOnAxis(ap=EIS[:, par, k:k + 1], axis=0)).then_inc(row_in[k], 16)

        def peer(l):
            for t in range(TT):
                pool.wait_ge(ei_done, l * TT + t + 1)
                gather((l * TT + t) * 2, u_exp[l])
                gather((l * TT + t) * 2 + 1, v_exp[l])

        for name, n in (("qkv", N_QKV), ("wo", N_WO), ("pq", N_PQ)):
            split_low(name, n)
        peer(0)
        for name, n in (("bcx", N_BCX), ("co", N_CO), ("pq1", N_PQ)):
            split_low(name, n)
        peer(1)

    @block.tensor
    def _(pe):
        mm = nc.tensor.matmul

        def modulation(name):
            g0 = RAW_AT[name] // RAW
            with pe.Fori(0, N_ADA // RAW) as i:
                for k in range(RAW):
                    pe.wait_ge(raw_in[k], i * 16 + 16 * (g0 + 1))
                    for j in range(DJ):
                        last = mm(PSf[:, bass.ds(i * (2 * RAW) + (6 * 512 + 2 * k), 2)], RW[:, k, j], CS[:, j],
                                  start=(j == 0), stop=(j == DJ - 1))
                    last.then_inc(raw_used, 1)

        def variance(n):
            for j in range(DJ):
                pe.wait_ge(sq_done, n * DJ + j + 1)
                mm(PSf[:, 2048:2048 + NS], MEAN, H[:, j, 0:NS], start=(j == 0), stop=(j == DJ - 1))
                last = mm(PSf[:, 2560:2560 + NP], MEAN, H[:, j, NS:NT], start=(j == 0), stop=(j == DJ - 1))
            last.then_inc(var_done, 1)

        def chunk_product(k):
            for j in range(DJ):
                for n, (w, a) in enumerate(((SH, HH), (SH, HL), (SL, HH))):
                    st, sp_ = (j == 0 and n == 0), (j == DJ - 1 and n == 2)
                    mm(PSf[:, (k % 2) * 1024:(k % 2) * 1024 + NS], w[:, k % 2, j], a[:, j, 0:NS], start=st, stop=sp_)
                    last = mm(PSf[:, (k % 2) * 1024 + NS:(k % 2) * 1024 + NT], w[:, k % 2, j], a[:, j, NS:NT],
                              start=st, stop=sp_)
            return last

        def chunk_product_tokens(k):
            for t in range(TT):
                for j in range(DJ):
                    for n, (w, a) in enumerate(((SH, HH), (SH, HL), (SL, HH))):
                        last = mm(PSf[:, (k % 2) * 1024 + t * P:(k % 2) * 1024 + (t + 1) * P],
                                  a[:, j, t * P:(t + 1) * P], w[:, k % 2, j],
                                  start=(j == 0 and n == 0), stop=(j == DJ - 1 and n == 2))
            return last

        def wait_chunk(s, raw, k):
            pe.wait_ge(raw_used, raw + k + 1)
            pe.wait_ge(evac_done, s + k + 1)

        def project(name, n):
            with pe.Fori(0, n // RAW) as i:
                for k in range(RAW):
                    wait_chunk(i * RAW + SPLIT_AT[name], i * RAW + RAW_AT[name], k)
                    chunk_product(k).then_inc(proj_done, 1)

        pe.sem_inc(proj_done, 2)
        pe.wait_ge(const_in, 16)
        pe.wait_ge(cs_done, 1)
        modulation("ada")
        variance(0)
        pe.wait_ge(hl_done, DJ)
        project("qkv", 8)
        for k in range(RAW):
            wait_chunk(SPLIT_AT["qkv"] + 8, RAW_AT["qkv"] + 8, k)
            (chunk_product if k < 2 else chunk_product_tokens)(k).then_inc(proj_done, 1)

        for c in range(11):
            if c < 10:
                pe.wait_ge(hsq_done, c + 1)
                mm(PSf[:, (c % 2) * 1024:(c % 2) * 1024 + NS], HEADM, SQ[:, c % 2, 0:NS], start=True, stop=True)
                mm(PSf[:, (c % 2) * 1024 + NS:(c % 2) * 1024 + NT], HEADM, SQ[:, c % 2, NS:NT],
                   start=True, stop=True).then_inc(hvar_done, 1)
            if c > 0:
                pe.wait_ge(hq_done, c)
                if c > 2:
                    pe.wait_ge(hrope_done, c - 2)
                mm(PSf[:, 2048 + ((c - 1) % 2) * 512:2560 + ((c - 1) % 2) * 512], SWAP, BIG[:, c - 1, 0:NS],
                   start=True, stop=True).then_inc(hrot_done, 1)

        pe.wait_ge(hrope_done, 10)
        pe.wait_ge(cache_in, 32)
        for m in range(2):
            with pe.Fori(0, 4) as jj:
                j10 = jj * 10 + 40 * m
                pe.wait_ge(q_staged, jj + (4 * m + 1))
                for u in range(12):
                    if u < 10:
                        half, qt = u // 5, u % 5
                        a, b = half * HD, (half + 1) * HD
                        if u >= 2:
                            pe.wait_ge(exp_done, j10 + (u - 1))
                        q = QS[a:b, qt * P:(qt + 1) * P]
                        o = (u % 2) * 1024
                        if qt < 4:
                            mm(PSf[:, o:o + NS], q, BIG[a:b, 8 + m, 0:NS], start=True, stop=True)
                            last = mm(PSf[:, o + NS:o + NT], q, KC[a:b, m], start=True, stop=True)
                        else:
                            last = mm(PSf[:, o:o + NP], q, BIG[a:b, 8 + m, NS:NT], start=True, stop=True)
                        last.then_inc(score_done, 1)
                    if 1 <= u <= 10:
                        v = u - 1
                        pe.wait_ge(p_done, j10 + u)
                        if v >= 1:
                            pe.wait_ge(ptc_done, j10 + v)
                        for kt in range(5 if v % 5 < 4 else 1):
                            last = nc.tensor.transpose(PSf[:, 2048 + kt * P:2048 + (kt + 1) * P],
                                                       PR[:, v % 2, kt * P:(kt + 1) * P], ID)
                        last.then_inc(pt_done, 1)
                    if u >= 2:
                        v = u - 2
                        half, qt = v // 5, v % 5
                        pe.wait_ge(ptc_done, j10 + (v + 1))
                        if v == 0:
                            pe.wait_ge(oh_done, jj + (4 * m + 1))
                        out = PSf[half * HD:(half + 1) * HD, 3072 + qt * P:3072 + (qt + 1) * P]
                        n = 5 if qt < 4 else 1
                        for kt in range(n):
                            if qt == 4:
                                val = BIG[:, 10 + m, NS + half * HD:NS + (half + 1) * HD]
                            elif kt < 4:
                                val = BIG[:, 10 + m, kt * P + half * HD:kt * P + (half + 1) * HD]
                            else:
                                val = VC[:, m * P + half * HD:m * P + (half + 1) * HD]
                            last = mm(out, val, PT[:, v % 2, kt * P:(kt + 1) * P], start=(kt == 0), stop=(kt == n - 1))
                        last.then_inc(pv_done, 1)
        pe.wait_ge(act_lo, 1)
        project("wo", N_WO)

        def route_and_gather(l, name):
            variance(2 * l + 1)
            pe.wait_ge(hl_done, DJ * (2 * l + 2))
            project(name, N_PQ)
            pe.wait_ge(sk_in, 16 * (l + 1))
            pe.wait_ge(evac_done, 2 + SPLIT_AT[name] + N_PQ)
            for t in range(TT):
                n = l * TT + t
                if n > 0:
                    pe.wait_ge(route_read, n)
                for hc in range(HC):
                    last = mm(PSf[:, hc * P:(hc + 1) * P], BIG[:, hc, t * P:(t + 1) * P], SK[:, hc],
                              start=True, stop=True)
                last.then_inc(route_ps, 1)
                if n > 0:
                    pe.wait_ge(ht_done, n)
                for j in range(DJ):
                    last = nc.tensor.transpose(PSf[:, 2048 + j * P:2048 + (j + 1) * P], H[:, j, t * P:(t + 1) * P], ID)
                last.then_inc(ht_ps, 1)
                pe.wait_ge(acc_done, n + 1)
                for j in range(DJ):
                    last = nc.tensor.transpose(PSf[:, 3072 + j * P:3072 + (j + 1) * P], ACC[:, j * P:(j + 1) * P], ID)
                last.then_inc(yt_done, 1)

        route_and_gather(0, "pq")
        pe.wait_ge(peer_done, TT)
        modulation("ada1")
        variance(2)
        pe.wait_ge(hl_done, 3 * DJ)
        project("bcx", N_BCX)
        pe.wait_ge(act_lo, 2)
        project("co", N_CO)
        route_and_gather(1, "pq1")
        variance(4)

    @block.scalar
    def _(act):
        def split_high(name, g, k, s):
            act.wait_ge(raw_in[k], g * 16 + 16)
            act.wait_ge(proj_done, s + 1)
            nc.scalar.copy(SH[:, k % 2], RW[:, k]).then_inc(hi_done, 1)

        def split_all(name, n):
            with act.Fori(0, n // RAW) as i:
                for k in range(RAW):
                    split_high(name, i + RAW_AT[name] // RAW, k, i * RAW + (SPLIT_AT[name] + k))

        def norm(n):
            wait_x(act, n)
            for j in range(DJ):
                nc.scalar.square(H[:, j], X[:, j]).then_inc(sq_done, 1)
            act.wait_ge(var_done, n + 1)
            nc.scalar.activation(RR[:], PSf[:, 2048:2048 + NT], ACT.Sqrt, bias=EP[:]).then_inc(rt_done, 1)
            if n == 0:
                act.wait_ge(mod_done, 1)
            if n == 2:
                act.wait_ge(mod_done, 2)
            for j in range(DJ):
                act.wait_ge(xn_done, n * DJ + j + 1)
                if n == 4:
                    nc.scalar.activation(H[:, j], H[:, j], ACT.Copy, scale=GN[:, 4, j:j + 1]).then_inc(y_done, 1)
                    continue
                f = n % 2
                for s, (a, b) in enumerate(((NS, NT), (0, NS))):
                    nc.scalar.activation(H[:, j, a:b], H[:, j, a:b], ACT.Identity,
                                         scale=GS[:, f, j, s:s + 1], bias=M[:, 3 * f * DJ + j, s:s + 1])
                act.drain()
                nc.scalar.copy(HH[:, j], H[:, j]).then_inc(h_done, 1)

        act.wait_ge(eps_done, 1)
        act.wait_ge(small_in, 16 * 5)
        nc.scalar.activation(CS[:], CS[:], ACT.Silu).then_inc(cs_done, 1)
        act.dma_start(SK[:], subk[0]).then_inc(sk_in, 16)
        norm(0)
        act.wait_ge(hl_done, DJ)
        act.dma_start(KC[:], kcache).then_inc(cache_in, 16)
        act.dma_start(VC[:], vcache).then_inc(cache_in, 16)
        split_all("qkv", N_QKV)

        act.wait_ge(evac_done, 2 + N_QKV)
        act.dma_start(v_new, BIG[:, 10:12, NS:NT]).then_inc(out_done, 16)
        for c in range(11):
            if c < 10:
                if c >= 2:
                    act.wait_ge(hvar_done, c - 1)
                nc.scalar.square(SQ[:, c % 2], BIG[:, c]).then_inc(hsq_done, 1)
            if c >= 1:
                act.wait_ge(hvar_done, c)
                if c > 2:
                    act.wait_ge(hq_done, c - 2)
                nc.scalar.activation(RN[:, (c - 1) % 2], ps_pair((c - 1) % 2), ACT.Sqrt, bias=EP[:]).then_inc(hrt_done, 1)
        act.wait_ge(hrope_done, 10)
        act.dma_start(k_new, BIG[:, 8:10, NS:NT]).then_inc(out_done, 16)

        for m in range(2):
            with act.Fori(0, 4) as jj:
                j10 = jj * 10 + 40 * m
                nc.scalar.mul(QS[:], BIG[:, bass.ds(jj + 4 * m, 1)].rearrange("p o n -> p (o n)"), HD ** -0.5).then_inc(q_staged, 1)
                for u in range(11):
                    if u < 10:
                        w = NT if u % 5 < 4 else NP
                        act.wait_ge(nb_done, j10 + (u + 1))
                        nc.scalar.activation(PR[:, u % 2, 0:w], PSf[:, (u % 2) * 1024:(u % 2) * 1024 + w], ACT.Exp,
                                             bias=NB[:, u % 2:u % 2 + 1],
                                             accum_out=RS[:, u % 2:u % 2 + 1]).then_inc(exp_done, 1)
                    if u >= 1:
                        v = u - 1
                        w = NT if v % 5 < 4 else NP
                        act.wait_ge(pt_done, j10 + u)
                        if v >= 2:
                            act.wait_ge(pv_done, j10 + (v - 1))
                        nc.scalar.copy(PT[:, v % 2, 0:w], PSf[:, 2048:2048 + w]).then_inc(ptc_done, 1)
                act.wait_ge(pv_done, j10 + 10)
                nc.scalar.copy(HH[:, bass.ds(jj + 4 * m, 1)].rearrange("p o n -> p (o n)"),
                               PSf[:, 3072:3072 + NT]).then_inc(o_done, 1)
        split_all("wo", N_WO)

        def gathers(l, name):
            norm(2 * l + 1)
            split_all(name, N_PQ)
            for t in range(TT):
                n = l * TT + t
                act.wait_ge(ht_ps, n + 1)
                if n > 0:
                    act.wait_ge(a_done, n)
                nc.scalar.copy(HTOK[:], PSf[:, 2048:3072]).then_inc(ht_done, 1)
                act.wait_ge(sm_in, n + 1)
                nc.scalar.activation(G[:], G[:], ACT.Exp).then_inc(sm_out, 1)
                if t == TT - 1 and l == 0:
                    act.wait_ge(route_ps, TT)
                    act.dma_start(SK[:], subk[1]).then_inc(sk_in, 16)
                act.wait_ge(a_done, n + 1)
                nc.scalar.activation(AA[:], AA[:], ACT.Gelu_apprx_tanh).then_inc(g_done, 1)

        gathers(0, "pq")
        norm(2)
        split_all("bcx", N_BCX)
        act.wait_ge(evac_done, 2 + SPLIT_AT["co"])
        for j in range(DJ):
            last = nc.scalar.copy(HH[:, j], BIG[:, j])
        last.then_inc(act_hi, 1)
        split_all("co", N_CO)
        gathers(1, "pq1")
        norm(4)
        act.wait_ge(y_done, DJ)
        act.dma_start(yT, H[:]).then_inc(out_done, 16)
        act.wait_ge(out_done, 48)

    @block.vector
    def _(dve):
        v = nc.vector

        def modulation(l):
            name = "ada1" if l else "ada"
            dve.wait_ge(raw_used, RAW_AT[name] + N_ADA)
            v.tensor_tensor(M[:], PSf[:, 3072:3072 + 96].rearrange("p (c s) -> p c s", s=2),
                            BA[:, l].unsqueeze(2).to_broadcast([P, N_ADA, 2]), ALU.add)
            dve.drain()
            for f in range(2):
                last = v.scalar_tensor_tensor(GS[:, f], M[:, (3 * f + 1) * DJ:(3 * f + 2) * DJ], 1.0,
                                              GN[:, 2 * l + f].unsqueeze(2).to_broadcast([P, DJ, 2]), ALU.add, ALU.mult)
            last.then_inc(mod_done, 1)

        def norm(n):
            dve.wait_ge(rt_done, n + 1)
            v.reciprocal(RR[:], RR[:])
            dve.drain()
            for j in range(DJ):
                v.tensor_tensor(H[:, j], X[:, j], RR[:], ALU.mult).then_inc(xn_done, 1)
            if n == 4:
                return
            for j in range(DJ):
                dve.wait_ge(h_done, (n if n < 4 else 0) * DJ + j + 1)
                v.tensor_tensor(HL[:, j], H[:, j], HH[:, j].bitcast(F32), ALU.subtract).then_inc(hl_done, 1)

        def copy_out(name, n):
            with dve.Fori(0, n // RAW) as i:
                for k in range(RAW):
                    dve.wait_ge(proj_done, i * RAW + (SPLIT_AT[name] + k + 3))
                    v.tensor_copy(BIG[:, bass.ds(i * RAW + k, 1)].rearrange("p o n -> p (o n)"),
                                  ps_pair(k % 2)).then_inc(evac_done, 1)

        def gate_scalar(i, k, f, s):
            return M[:].rearrange("p c s -> p (c s)")[:, bass.ds(i * (2 * RAW) + (2 * (3 * f + 2) * DJ + 2 * k + s), 1)]

        def residual_out(name, n):
            with dve.Fori(0, n // RAW) as i:
                for k in range(RAW):
                    dve.wait_ge(proj_done, i * RAW + (SPLIT_AT[name] + k + 3))
                    for s, (a, b) in enumerate(((NS, NT), (0, NS))):
                        x = X[:, bass.ds(i * RAW + k, 1), a:b].rearrange("p o n -> p (o n)")
                        last = v.scalar_tensor_tensor(x, ps_pair(k % 2)[:, a:b], gate_scalar(i, k, 0, s), x,
                                                      ALU.mult, ALU.add)
                    last.then_inc(evac_done, 1)

        def top16(vals, idx, src, wk, n, after_read=None):
            for i in range(n):
                v.max(vals[:, i, 0:8], src(i))
            dve.drain()
            for i in range(n):
                v.max_index(idx[:, i, 0:8], vals[:, i, 0:8], src(i))
                last = v.match_replace(wk(i), vals[:, i, 0:8], src(i), LOWEST)
            if after_read is not None:
                last.then_inc(after_read, 1)
            dve.drain()
            for i in range(n):
                v.max(vals[:, i, 8:16], wk(i))
            dve.drain()
            for i in range(n):
                v.max_index(idx[:, i, 8:16], vals[:, i, 8:16], wk(i))
            dve.drain()

        def route(n):
            dve.wait_ge(route_ps, n + 1)
            top16(V16, I16, lambda i: PSf[:, i * P:(i + 1) * P], lambda i: WK[:, i], HC, route_read)
            v.tensor_copy(IF[:], I16[:])
            vv = V16[:].rearrange("p (h c) k -> p h c k", c=2)
            v.tensor_tensor(CAND[:], vv[:, :, 0].unsqueeze(3).to_broadcast([P, PH, TOPK, TOPK]),
                            vv[:, :, 1].unsqueeze(2).to_broadcast([P, PH, TOPK, TOPK]), ALU.add)
            dve.drain()
            cf = CAND[:].rearrange("p h a b -> p h (a b)")
            wf = WK[:].rearrange("p (h c) n -> p h (c n)", c=2)
            top16(TS, PO, lambda i: cf[:, i], lambda i: wf[:, i], PH)
            po = PO[:].rearrange("p h k -> p (h k)")
            v.tensor_scalar(AB[:, 0], po, 4, None, ALU.logical_shift_right)
            v.tensor_scalar(AB[:, 1], po, 15, None, ALU.bitwise_and)
            v.tensor_tensor(G[:], TS[:], TS[:, :, 0:1].to_broadcast([P, PH, TOPK]), ALU.subtract).then_inc(sm_in, 1)
            dve.drain()
            v.tensor_copy(ABF[:], AB[:])
            dve.drain()
            fi = IF[:].rearrange("p (h c) k -> p h c k", c=2)
            for c in range(2):
                v.tensor_tensor(EQ[:], ABF[:, c].unsqueeze(2).to_broadcast([P, PICKS, TOPK]),
                                J16.unsqueeze(1).to_broadcast([P, PICKS, TOPK]), ALU.is_equal)
                dve.drain()
                e4 = EQ[:].rearrange("p (h k) j -> p h k j", k=TOPK)
                v.tensor_tensor(e4, e4, fi[:, :, c].unsqueeze(2).to_broadcast([P, PH, TOPK, TOPK]), ALU.mult)
                dve.drain()
                v.tensor_reduce(I12[:, c], EQ[:], AX_X, ALU.add)
                dve.drain()
            v.scalar_tensor_tensor(EI[:], I12[:, 0], float(NKEY), I12[:, 1], ALU.mult, ALU.add).then_inc(ei_done, 1)
            dve.wait_ge(sm_out, n + 1)
            v.tensor_reduce(Z[:], G[:], AX_X, ALU.add)
            dve.drain()
            v.reciprocal(Z[:], Z[:])
            dve.drain()
            v.tensor_tensor(G[:], G[:], Z[:].unsqueeze(2).to_broadcast([P, PH, TOPK]), ALU.mult)

        def wait_row(i, call, k):
            dve.wait_ge(row_in[k % 8], i * 32 + 16 * (call * (PICKS // 8) + k // 8 + 1))

        def gathered(n, t):
            call = 2 * n
            dve.wait_ge(ht_done, n + 1)
            with dve.Fori(0, PICKS // 16) as i:
                for k in range(16):
                    wait_row(i, call, k)
                    v.tensor_tensor_reduce(ROWS[:, k % 8], ROWS[:, k % 8], HTOK[:], 1.0, 0.0, ALU.mult, ALU.add,
                                           A16[:, k:k + 1]).then_inc(row_used, 1)
                dve.drain()
                v.tensor_copy(AA[:, bass.ds(i * 16, 16)], A16[:])
                dve.drain()
            dve.drain().then_inc(a_done, 1)
            if n > 0:
                dve.wait_ge(yt_done, n)
            v.memset(ACC[:], 0.0)
            dve.wait_ge(g_done, n + 1)
            v.tensor_tensor(WW[:], AA[:], G[:].rearrange("p h k -> p (h k)"), ALU.mult)
            dve.drain()
            call += 1
            with dve.Fori(0, PICKS // 16) as i:
                for k in range(16):
                    wait_row(i, call, k)
                    v.scalar_tensor_tensor(ACC[:], ROWS[:, k % 8], WW[:, bass.ds(i * 16 + k, 1)], ACC[:],
                                           ALU.mult, ALU.add).then_inc(row_used, 1)
                    dve.drain()
            dve.drain().then_inc(acc_done, 1)
            dve.wait_ge(yt_done, n + 1)
            s = 0 if t == TT - 1 else 1
            for j in range(DJ):
                x = X[:, j, t * P:(t + 1) * P]
                last = v.scalar_tensor_tensor(x, PSf[:, 3072 + j * P:3072 + (j + 1) * P],
                                              M[:, 5 * DJ + j, s:s + 1], x, ALU.mult, ALU.add)
            last.then_inc(peer_done, 1)

        dve.sem_inc(evac_done, 2)
        dve.sem_inc(row_used, RING)
        dve.sem_inc(oh_done, 1)
        v.memset(EP[:], EPS).then_inc(eps_done, 1)
        dve.wait_ge(small_in, 16 * 5)
        modulation(0)
        norm(0)
        copy_out("qkv", N_QKV)
        for c in range(11):
            if c < 10:
                dve.wait_ge(hrt_done, c + 1)
                v.reciprocal(RN[:, c % 2], RN[:, c % 2])
                dve.drain()
                v.scalar_tensor_tensor(BIG[:, c], BIG[:, c], HG[:, c:c + 1], RN[:, c % 2],
                                       ALU.mult, ALU.mult).then_inc(hq_done, 1)
            if c >= 1:
                b = c - 1
                dve.wait_ge(hrot_done, c)
                v.tensor_tensor(TR[:, b % 2], PSf[:, 2048 + (b % 2) * 512:2560 + (b % 2) * 512], SIN, ALU.mult)
                v.tensor_tensor(BIG[:, b, 0:NS], BIG[:, b, 0:NS], COS, ALU.mult)
                dve.drain()
                v.tensor_tensor(BIG[:, b, 0:NS], BIG[:, b, 0:NS], TR[:, b % 2], ALU.add).then_inc(hrope_done, 1)

        for m in range(2):
            with dve.Fori(0, 4) as jj:
                j10 = jj * 10 + 40 * m
                for u in range(11):
                    if u < 10:
                        w = NT if u % 5 < 4 else NP
                        dve.wait_ge(score_done, j10 + (u + 1))
                        v.reduce_max(MX[:, u % 2:u % 2 + 1], PSf[:, (u % 2) * 1024:(u % 2) * 1024 + w], AX_X)
                        dve.drain()
                        v.tensor_scalar(NB[:, u % 2:u % 2 + 1], MX[:, u % 2:u % 2 + 1], -1.0, None,
                                        ALU.mult).then_inc(nb_done, 1)
                    if u >= 1:
                        b = u - 1
                        w = NT if b % 5 < 4 else NP
                        dve.wait_ge(exp_done, j10 + u)
                        v.reciprocal(RI[:, b % 2:b % 2 + 1], RS[:, b % 2:b % 2 + 1])
                        dve.drain()
                        v.tensor_scalar(PR[:, b % 2, 0:w], PR[:, b % 2, 0:w], RI[:, b % 2:b % 2 + 1], None,
                                        ALU.mult).then_inc(p_done, 1)
                dve.wait_ge(o_done, jj + (4 * m + 1))
                v.tensor_tensor(HL[:, bass.ds(jj + 4 * m, 1)].rearrange("p o n -> p (o n)"), PSf[:, 3072:3072 + NT],
                                HH[:, bass.ds(jj + 4 * m, 1)].rearrange("p o n -> p (o n)").bitcast(F32),
                                ALU.subtract).then_inc(oh_done, 1)
        dve.drain().then_inc(act_lo, 1)
        residual_out("wo", N_WO)
        norm(1)
        dve.wait_ge(out_done, 32)
        copy_out("pq", N_PQ)
        for t in range(TT):
            route(t)
            gathered(t, t)

        modulation(1)
        norm(2)
        with dve.Fori(0, 2) as i:
            for q in range(12):
                jl, part = q // 3, q % 3
                dve.wait_ge(proj_done, i * 12 + (SPLIT_AT["bcx"] + q + 3))
                ps = ps_pair(q % 2)
                cv = CV[:].rearrange("p j t -> p (j t)")

                def tap(n):
                    return cv[:, bass.ds(i * 16 + (jl * 4 + n), 1)]
                if part == 0:
                    v.tensor_copy(GC[:], ps).then_inc(evac_done, 1)
                    dve.drain()
                elif part == 1:
                    v.tensor_tensor(UU[:], GC[:], ps, ALU.mult).then_inc(evac_done, 1)
                    dve.drain()
                    v.tensor_scalar(CC[:], UU[:], tap(1), tap(3), ALU.mult, ALU.add)
                    dve.drain()
                    for a, b in ((0, NS), (NS, NT)):
                        v.scalar_tensor_tensor(CC[:, a + 1:b], UU[:, a:b - 1], tap(0), CC[:, a + 1:b], ALU.mult, ALU.add)
                    dve.drain()
                    for a, b in ((0, NS), (NS, NT)):
                        v.scalar_tensor_tensor(CC[:, a:b - 1], UU[:, a + 1:b], tap(2), CC[:, a:b - 1], ALU.mult, ALU.add)
                    dve.drain()
                else:
                    v.tensor_tensor(BIG[:, bass.ds(i * 4 + jl, 1)].rearrange("p o n -> p (o n)"), CC[:], ps,
                                    ALU.mult).then_inc(evac_done, 1)
                    dve.drain()
        dve.wait_ge(act_hi, 1)
        for j in range(DJ):
            last = v.tensor_tensor(HL[:, j], BIG[:, j], HH[:, j].bitcast(F32), ALU.subtract)
        last.then_inc(act_lo, 1)
        residual_out("co", N_CO)
        norm(3)
        copy_out("pq1", N_PQ)
        for t in range(TT):
            route(TT + t)
            gathered(TT + t, t)
        norm(4)

    block_cm.__exit__(None, None, None)


def _constants():
    c = np.zeros((P, C_ALL), np.float32)
    p = np.arange(P)
    c[:, C_MEAN:C_MEAN + P] = 1.0 / D
    c[:, C_HEAD:C_HEAD + P] = (p[:, None] // HD == p[None, :] // HD) / np.float32(HD)
    c[:, C_SWAP:C_SWAP + P] = p[:, None] == (p[None, :] ^ 16)
    c[:, C_ID:C_ID + P] = np.eye(P)
    c[:, C_J16:C_J16 + 16] = np.arange(16)
    axis = HD // 2
    inv = (np.float32(10000.0) ** (-np.arange(0, axis, 2, dtype=np.float32) / np.float32(axis))).astype(np.float32)
    t = np.arange(NS)
    place = np.where((p % HD < axis)[:, None], (t // GRID_W)[None, :], (t % GRID_W)[None, :]).astype(np.float32)
    ang = (place * inv[p % 16][:, None]).astype(np.float32)
    c[:, C_COS:C_COS + NS] = np.cos(ang)
    c[:, C_SIN:C_SIN + NS] = np.sin(ang) * np.where(p % 32 < 16, -1.0, 1.0)[:, None]
    return c


def kernel(x_prompt, x_sample, cache_k, cache_v, c, c_ctx, w_ada, b_ada, norm_mix, norm_ffn, norm_final,
           w_qkv, q_gain, k_gain, w_o, w_bcx, conv_w, conv_b, w_conv_out, w_pq, sub_keys, u_exp, v_exp):
    import concourse.bacc as _bacc
    from concourse.bass_utils import run_bass_kernel_spmd as _run

    def cols(w):
        return np.ascontiguousarray(w.reshape(DJ, P, -1, P).transpose(2, 1, 0, 3))

    a = {k: np.asarray(v) for k, v in locals().items() if isinstance(v, (np.ndarray,)) or hasattr(v, "__array__")}
    heads = [(j // 4) * 8 + half * 4 + j % 4 for j in range(8) for half in range(2)]
    wqkv = a["w_qkv"][0]
    wq = wqkv[:, :HEADS * HD].reshape(D, HEADS, HD)[:, heads].reshape(D, D)
    wo = a["w_o"][0].reshape(HEADS, HD, D)[heads].reshape(D, D)
    bcx = cols(a["w_bcx"][0]).reshape(3, DJ, P, DJ, P)
    bcx = bcx[[1, 2, 0]].transpose(1, 0, 2, 3, 4).reshape(N_BCX, P, DJ, P)
    stream = np.concatenate([
        cols(a["w_ada"][0]), cols(wq), cols(wqkv[:, HEADS * HD:]), cols(wo), cols(a["w_pq"][0]),
        cols(a["w_ada"][1]), bcx, cols(a["w_conv_out"][0]), cols(a["w_pq"][1])])
    x = np.concatenate([a["x_sample"][0], a["x_prompt"][0]])
    by_chunk = lambda m: np.ascontiguousarray(m.reshape(m.shape[:-1] + (DJ, P)))
    ins = {
        "xT": np.ascontiguousarray(x.reshape(NT, DJ, P).transpose(2, 1, 0)),
        "cond": np.ascontiguousarray(np.stack([a["c_ctx"], a["c"][0]]).reshape(2, DJ, P).transpose(2, 1, 0)),
        "consts": _constants(),
        "wstream": stream,
        "bada": np.ascontiguousarray(a["b_ada"].reshape(DEPTH, N_ADA, P).transpose(2, 0, 1)),
        "gains": np.ascontiguousarray(by_chunk(np.stack([a["norm_mix"][0], a["norm_ffn"][0], a["norm_mix"][1],
                                                         a["norm_ffn"][1], a["norm_final"]])).transpose(2, 0, 1)),
        "hgain": np.ascontiguousarray(np.stack([np.concatenate([g, g]) for g in
                                                [a["q_gain"][0]] * 8 + [a["k_gain"][0]] * 2]).T),
        "convp": np.ascontiguousarray(by_chunk(np.concatenate([a["conv_w"][0], a["conv_b"]])).transpose(2, 1, 0)),
        "kcache": np.ascontiguousarray(a["cache_k"][0, 0].reshape(P, 2, P).transpose(2, 1, 0)),
        "vcache": np.ascontiguousarray(a["cache_v"][0, 0].reshape(P, 2 * P)),
        "subk": np.ascontiguousarray(a["sub_keys"].reshape(DEPTH, HC, NKEY, P).transpose(0, 3, 1, 2)),
        "u_exp0": a["u_exp"][0], "u_exp1": a["u_exp"][1], "v_exp0": a["v_exp"][0], "v_exp1": a["v_exp"][1],
    }
    outs = {"yT": (P, DJ, NT), "k_new": (P, 2, NP), "v_new": (P, 2, NP)}
    nc = _bacc.Bacc("TRN2", target_bir_lowering=False, num_devices=1)
    ap = {n: nc.dram_tensor(n, v.shape, F32, kind="ExternalInput").ap() for n, v in ins.items()}
    op = {n: nc.dram_tensor(n, s, F32, kind="ExternalOutput").ap() for n, s in outs.items()}
    hybrid_step(nc, ap["xT"], ap["cond"], ap["consts"], ap["wstream"], ap["bada"], ap["gains"], ap["hgain"],
                ap["convp"], ap["kcache"], ap["vcache"], ap["subk"], [ap["u_exp0"], ap["u_exp1"]],
                [ap["v_exp0"], ap["v_exp1"]], op["yT"], op["k_new"], op["v_new"])
    r = _run(nc, [ins], core_ids=[0]).results[0]
    y = r["yT"].transpose(2, 1, 0).reshape(NT, D)
    k = r["k_new"].transpose(2, 1, 0).reshape(1, 1, NP, KVH, HD)
    v = r["v_new"].reshape(1, 1, NP, KVH, HD)
    return (np.ascontiguousarray(y[NS:])[None], np.ascontiguousarray(y[:NS])[None],
            np.ascontiguousarray(k), np.ascontiguousarray(v))
```

```python
import math

import numpy as np

import concourse.bass as bass
from concourse import mybir

P = 128
ALU = mybir.AluOpType
ACT = mybir.ActivationFunctionType
F32 = mybir.dt.float32
F32R = mybir.dt.float32r
U32 = mybir.dt.uint32
AX_X = mybir.AxisListType.X

D = 1024
DJ = D // P
NS = 512
NP = 128
NT = NS + NP
TT = NT // P
DEPTH = 2
HEADS, KVH, HD = 16, 4, 64
GRID_W = 64
PH, NKEY, TOPK = 8, 128, 16
HC = PH * 2
PICKS = PH * TOPK
EPS = 1e-6
LOWEST = -3.0e38

RAW = 4
NB_E = NKEY
TG = 64
N_ADA, N_QKV, N_WO, N_PQ, N_BCX, N_CO = 48, 12, 8, 16, 24, 8
STREAM = [("ada", N_ADA), ("qkv", N_QKV), ("wo", N_WO), ("pq", N_PQ), ("ada1", N_ADA), ("dense0", 2 * NB_E),
          ("bcx", N_BCX), ("co", N_CO), ("pq1", N_PQ), ("dense1", 2 * NB_E)]
RAW_AT, SPLIT_AT, PROJ_AT = {}, {}, {}
_raw = _split = _proj = 0
for _name, _n in STREAM:
    RAW_AT[_name], SPLIT_AT[_name], PROJ_AT[_name] = _raw, _split, _proj
    _raw += _n
    _split += 0 if _name.startswith("ada") else _n
    _proj += 0 if _name.startswith(("ada", "dense")) else _n
RING = 4

C_MEAN, C_HEAD, C_SWAP, C_ID, C_IOTA, C_COS, C_SIN = 0, 128, 256, 384, 512, 640, 1152
C_ALL = 1664


def hybrid_step(nc, xT, cond, consts, wstream, bada, gains, hgain, convp, kcache, vcache, subk,
                u_exp, v_exp, u_blocks, v_blocks, g_dram, yT, k_new, v_new):
    off = [16512]

    def sb(name, shape, dt, at=None):
        size = int(np.prod(shape[1:])) * 4
        if at is None:
            at = off[0]
            off[0] += size
        return nc.alloc_sbuf_tensor_at(name, shape, dt, offset=at), at

    X, _ = sb("X", [P, DJ, NT], F32)
    H, at_H = sb("H", [P, DJ, NT], F32)
    HH, at_HH = sb("HH", [P, DJ, NT], F32R)
    HL, _ = sb("HL", [P, DJ, NT], F32R)
    BIG, at_BIG = sb("BIG", [P, HC, NT], F32)
    RW, at_RW = sb("RW", [P, RAW, DJ, P], F32)
    SH, _ = sb("SH", [P, 2, DJ, P], F32R)
    SL, _ = sb("SL", [P, 2, DJ, P], F32R)
    SK, _ = sb("SK", [P, HC, NKEY], F32)
    CO, _ = sb("CO", [P, C_ALL], F32)
    CAND, at_CAND = sb("CAND", [P, PH, TOPK, TOPK], F32)
    WK, at_WK = sb("WK", [P, HC, NKEY], F32)
    HTOK, _ = sb("HTOK", [P, D], F32)
    ACC, _ = sb("ACC", [P, D], F32)
    small, _ = sb("small", [P, 768], F32)
    at_small = [off[0] - 3072]

    def tiny(name, n, dt=F32, shape=None):
        t, _ = sb(name, shape or [P, n], dt, at=at_small[0])
        at_small[0] += 32 * -(-n // 8)
        return t

    CS = tiny("CS", 16, shape=[P, DJ, 2])
    M = tiny("M", 192, shape=[P, DEPTH, N_ADA, 2])
    GS = tiny("GS", 64, shape=[P, DEPTH, 2, DJ, 2])
    BA = tiny("BA", 96, shape=[P, DEPTH, N_ADA])
    GN = tiny("GN", 40, shape=[P, 5, DJ])
    HG = tiny("HG", 10)
    CV = tiny("CV", 32, shape=[P, DJ, 4])
    EP = tiny("EP", 1)
    MX = tiny("MX", 2)
    NB = tiny("NB", 2)
    RS = tiny("RS", 2)
    RI = tiny("RI", 2)
    A16 = tiny("A16", 16)
    Z = tiny("Z", 8)
    assert at_small[0] <= off[0]
    V16, _ = sb("V16", [P, HC, TOPK], F32)
    I16, _ = sb("I16", [P, HC, TOPK], U32)
    IF, _ = sb("IF", [P, HC, TOPK], F32)
    TS, _ = sb("TS", [P, PH, TOPK], F32)
    PO, _ = sb("PO", [P, PH, TOPK], U32)
    AB, _ = sb("AB", [P, 2, PICKS], U32)
    ABF, _ = sb("ABF", [P, 2, PICKS], F32)
    I12, _ = sb("I12", [P, 2, PICKS], F32)
    EI, _ = sb("EI", [P, PICKS], U32)
    EIS, _ = sb("EIS", [P, 2, 4], U32)
    G, _ = sb("G", [P, PH, TOPK], F32)
    AA, _ = sb("AA", [P, PICKS], F32)
    WW, _ = sb("WW", [P, PICKS], F32)
    ROWS, _ = sb("ROWS", [P, RING, D], F32, at=at_BIG)
    WH, _ = sb("WH", [P, 4, NS], F32R, at=at_BIG + 16384)
    WL, _ = sb("WL", [P, 4, NS], F32R, at=at_BIG + 24576)
    GB, _ = sb("GB", [P, 4, NS], F32, at=at_BIG + 32768)
    VH, _ = sb("VH", [P, 4, DJ, P], F32R, at=at_H)
    GE, _ = sb("GE", [P, 2, NS], F32, at=at_H + 16384)
    VL, _ = sb("VL", [P, 4, DJ, P], F32R, at=at_CAND)
    PK, _ = sb("PK", [P, 4, 3, P], F32, at=at_H)
    OH, _ = sb("OH", [P, 2, 4, 2, P], F32, at=at_H + 4 * 3 * P * 4)
    GT, _ = sb("GT", [P, NKEY, TG], F32, at=at_RW)
    EQ, _ = sb("EQ", [P, PICKS, TOPK], F32, at=at_WK)
    SQ, _ = sb("SQ", [P, 2, NT], F32, at=at_H)
    RN, _ = sb("RN", [P, 2, NT], F32, at=at_H + 2 * NT * 4)
    TR, _ = sb("TR", [P, 2, NS], F32, at=at_H + 4 * NT * 4)
    QS, _ = sb("QS", [P, NT], F32, at=at_H)
    PR, _ = sb("PR", [P, 2, NT], F32, at=at_H + NT * 4)
    PT, _ = sb("PT", [P, 2, NT], F32, at=at_H + 3 * NT * 4)
    KC, _ = sb("KC", [P, 2, P], F32, at=at_CAND)
    VC, _ = sb("VC", [P, 2 * P], F32, at=at_CAND + 1024)
    GC, _ = sb("GC", [P, NT], F32, at=at_WK)
    UU, _ = sb("UU", [P, NT], F32, at=at_WK + 2560)
    CC, _ = sb("CC", [P, NT], F32, at=at_CAND)
    RR, _ = sb("RR", [P, NT], F32, at=at_CAND + 2560)

    PS = nc.alloc_psum_tensor("PS", [P, 8, 512], F32)
    PSf = PS[:].rearrange("p b n -> p (b n)")

    def ps_pair(par):
        return PSf[:, par * 1024:par * 1024 + NT]

    MEAN, HEADM, SWAP, ID = (CO[:, c:c + P] for c in (C_MEAN, C_HEAD, C_SWAP, C_ID))
    IOTA = CO[:, C_IOTA:C_IOTA + NKEY]
    J16 = IOTA[:, 0:TOPK]
    COS, SIN = CO[:, C_COS:C_COS + NS], CO[:, C_SIN:C_SIN + NS]

    sem = nc.alloc_semaphore
    x_in, small_in, const_in, cache_in = sem("x_in"), sem("small_in"), sem("const_in"), sem("cache_in")
    sk_in = sem("sk_in")
    raw_in = [sem(f"raw_in{k}") for k in range(RAW)]
    raw_used = sem("raw_used")
    hi_done = sem("hi_done")
    proj_done = sem("proj_done")
    evac_done = sem("evac_done")
    eps_done, cs_done, mod_done = sem("eps_done"), sem("cs_done"), sem("mod_done")
    sq_done, var_done, rt_done, xn_done = sem("sq_done"), sem("var_done"), sem("rt_done"), sem("xn_done")
    h_done, hl_done = sem("h_done"), sem("hl_done")
    hsq_done, hvar_done, hrt_done, hq_done, hrot_done, hrope_done = (
        sem(n) for n in ("hsq_done", "hvar_done", "hrt_done", "hq_done", "hrot_done", "hrope_done"))
    q_staged, score_done, nb_done, exp_done, p_done, pt_done, ptc_done, pv_done, o_done = (
        sem(n) for n in ("q_staged", "score_done", "nb_done", "exp_done", "p_done", "pt_done",
                         "ptc_done", "pv_done", "o_done"))
    oh_done = sem("oh_done")
    act_hi, act_lo = sem("act_hi"), sem("act_lo")
    route_ps, route_read = sem("route_ps"), sem("route_read")
    ht_ps, ht_done = sem("ht_ps"), sem("ht_done")
    sm_in, sm_out = sem("sm_in"), sem("sm_out")
    ei_done, stage_done = sem("ei_done"), sem("stage_done")
    row_in = [sem(f"row_in{k}") for k in range(RING)]
    rows_asked = sem("rows_asked")
    row_used = sem("row_used")
    a_done, g_done, acc_done, yt_done, peer_done = (
        sem(n) for n in ("a_done", "g_done", "acc_done", "yt_done", "peer_done"))
    y_done, out_done = sem("y_done"), sem("out_done")
    pick_ready, pick_ps, pick_done = sem("pick_ready"), sem("pick_ps"), sem("pick_done")
    oh_ready = sem("oh_ready")
    gq_done = sem("gq_done")
    gt_done = sem("gt_done")
    gw_done = sem("gw_done")
    gb_in = [sem(f"gb_in{k}") for k in range(4)]
    a_prod = sem("a_prod")
    gelu_done = sem("gelu_done")
    w_done = sem("w_done")
    wh_done = sem("wh_done")
    wl_done = sem("wl_done")
    v_prod = sem("v_prod")
    v_acc = sem("v_acc")

    NORMS = [("mod", 0), ("peer", 0), ("mod", 1), ("peer", 1), ("final", 0)]

    def wait_x(eng, n):
        if n == 0:
            eng.wait_ge(x_in, 16)
        elif n in (1, 3):
            last = PROJ_AT["pq"] if n == 1 else PROJ_AT["pq1"]
            eng.wait_ge(evac_done, 2 + last)
        else:
            eng.wait_ge(peer_done, n // 2)
            eng.wait_ge(v_acc, 4 + (n // 2) * (NB_E // 2) * DJ)

    block_cm = nc.Block()
    block = block_cm.__enter__()

    @block.sync
    def _(sp):
        sp.dma_start(CO[:], consts).then_inc(const_in, 16)
        sp.dma_start(CS[:], cond).then_inc(small_in, 16)
        sp.dma_start(BA[:], bada).then_inc(small_in, 16)
        sp.dma_start(GN[:], gains).then_inc(small_in, 16)
        sp.dma_start(HG[:], hgain).then_inc(small_in, 16)
        sp.dma_start(CV[:], convp).then_inc(small_in, 16)
        sp.dma_start(X[:], xT).then_inc(x_in, 16)

        def chunk(c, k):
            sp.dma_start(RW[:, k], wstream[bass.ds(c, 1)].rearrange("o p j n -> (o p) j n")).then_inc(raw_in[k], 16)

        for k in range(RAW):
            chunk(k, k)

        def stream(first, last, skip):
            with sp.Fori(first // RAW, last // RAW) as g:
                for k in range(RAW):
                    sp.wait_ge(raw_used, g * RAW + (k + 1 - RAW))
                    chunk(g * RAW + (k - skip), k)

        def experts(l):
            for tg in range(NS // TG):
                sp.wait_ge(gt_done, 2 + (l * (NS // TG) + tg + 1) * (TG // 4))
                sp.dma_start(g_dram[:, :, tg * TG:(tg + 1) * TG].rearrange("i p t -> p i t"),
                             GT[:]).then_inc(gw_done, 16)
            sp.wait_ge(gw_done, 16 * (NS // TG) * (l + 1))
            r0 = RAW_AT[f"dense{l}"]

            def expert_chunk(src, b, i, r):
                sp.wait_ge(raw_used, i * 8 + (r0 + r + 1 - RAW))
                sp.dma_start(RW[:, r % RAW], src[bass.ds(b, 1)].rearrange("o p j n -> (o p) j n")
                             ).then_inc(raw_in[r % RAW], 16)

            def blocks(i, last=False):
                for k in range(4):
                    if not (last and k == 3):
                        expert_chunk(u_blocks[l], i * 4 + (k + 1), i, 2 * k + 1)
                    expert_chunk(v_blocks[l], i * 4 + k, i, 2 * k + (1 if last and k == 3 else 2))
                    sp.wait_ge(w_done, i * 4 + (l * NB_E + k + 1))
                    sp.dma_start(GB[:, k], g_dram[bass.ds(i * 4 + k, 1)].rearrange("o p t -> (o p) t")
                                 ).then_inc(gb_in[k], 16)

            expert_chunk(u_blocks[l], 0, 0, 0)
            with sp.Fori(0, NB_E // 4 - 1) as i:
                blocks(i)
            blocks(NB_E // 4 - 1, last=True)

        stream(RAW, RAW_AT["dense0"], 0)
        experts(0)
        stream(RAW_AT["bcx"], RAW_AT["dense1"], 2 * NB_E)
        experts(1)

    @block.gpsimd
    def _(pool):
        def split_low(name, n):
            s0 = SPLIT_AT[name]
            with pool.Fori(0, n // RAW) as i:
                for k in range(RAW):
                    pool.wait_ge(hi_done, i * RAW + (s0 + k + 1))
                    nc.gpsimd.tensor_tensor(SL[:, k % 2], RW[:, k], SH[:, k % 2].bitcast(F32),
                                            ALU.subtract).then_inc(raw_used, 1)

        def low(dst, r, upper, hi):
            pool.wait_ge(hi_done, hi)
            nc.gpsimd.tensor_tensor(dst, RW[:, r % RAW], upper.bitcast(F32), ALU.subtract).then_inc(raw_used, 1)

        def blocks(l, i, call, last=False):
            s0 = SPLIT_AT[f"dense{l}"]
            for k in range(4):
                n0 = call * PICKS
                table = (v_exp if call % 2 else u_exp)[l]
                if k % 2 == 0:
                    nc.gpsimd.tensor_copy(EIS[:, k // 2], EI[:, bass.ds((i - 16 * (call % 2)) * 8 + 2 * k, 4)]
                                          ).then_inc(stage_done, 1)
                    pool.wait_ge(stage_done, i * 2 + (l * 64 + k // 2 + 1))
                for q in (2 * k, 2 * k + 1):
                    pool.wait_ge(row_used, (i - 16 * (call % 2)) * 8 + (n0 + q + 1))
                    pool.sem_inc(rows_asked)
                    nc.gpsimd.indirect_dma_start(
                        ROWS[:, q % RING], None, table,
                        bass.IndirectOffsetOnAxis(ap=EIS[:, k // 2, q % 4:q % 4 + 1], axis=0)).then_inc(row_in[q % RING], 16)
                end = last and k == 3
                if not end:
                    low(SL[:, (k + 1) % 2], 2 * k + 1, SH[:, (k + 1) % 2], i * 8 + (s0 + 2 * k + 2))
                low(VL[:, k], 2 * k + (1 if end else 2), VH[:, k], i * 8 + (s0 + 2 * k + (2 if end else 3)))

        def experts(l):
            pool.wait_ge(ei_done, l + 1)
            pool.wait_ge(pick_done, 4 * (l + 1))
            low(SL[:, 0], 0, SH[:, 0], SPLIT_AT[f"dense{l}"] + 1)
            with pool.Fori(0, 16) as i:
                blocks(l, i, 2 * l)
            with pool.Fori(16, 31) as i:
                blocks(l, i, 2 * l + 1)
            blocks(l, 31, 2 * l + 1, last=True)

        for name, n in (("qkv", N_QKV), ("wo", N_WO), ("pq", N_PQ)):
            split_low(name, n)
        experts(0)
        for name, n in (("bcx", N_BCX), ("co", N_CO), ("pq1", N_PQ)):
            split_low(name, n)
        experts(1)

    @block.tensor
    def _(pe):
        mm = nc.tensor.matmul

        def modulation(name, first=0, end=N_ADA):
            g0 = RAW_AT[name] // RAW
            with pe.Fori(first // RAW, end // RAW) as i:
                for k in range(RAW):
                    pe.wait_ge(raw_in[k], i * 16 + 16 * (g0 + 1))
                    for j in range(DJ):
                        last = mm(PSf[:, bass.ds(i * (2 * RAW) + (6 * 512 + 2 * k), 2)], RW[:, k, j], CS[:, j],
                                  start=(j == 0), stop=(j == DJ - 1))
                    last.then_inc(raw_used, 1)

        def variance(n):
            for j in range(DJ):
                pe.wait_ge(sq_done, n * DJ + j + 1)
                mm(PSf[:, 2048:2048 + NS], MEAN, H[:, j, 0:NS], start=(j == 0), stop=(j == DJ - 1))
                last = mm(PSf[:, 2560:2560 + NP], MEAN, H[:, j, NS:NT], start=(j == 0), stop=(j == DJ - 1))
            last.then_inc(var_done, 1)

        def chunk_product(k):
            for j in range(DJ):
                for n, (w, a) in enumerate(((SH, HH), (SH, HL), (SL, HH))):
                    st, sp_ = (j == 0 and n == 0), (j == DJ - 1 and n == 2)
                    mm(PSf[:, (k % 2) * 1024:(k % 2) * 1024 + NS], w[:, k % 2, j], a[:, j, 0:NS], start=st, stop=sp_)
                    last = mm(PSf[:, (k % 2) * 1024 + NS:(k % 2) * 1024 + NT], w[:, k % 2, j], a[:, j, NS:NT],
                              start=st, stop=sp_)
            return last

        def chunk_product_tokens(k):
            for t in range(TT):
                for j in range(DJ):
                    for n, (w, a) in enumerate(((SH, HH), (SH, HL), (SL, HH))):
                        last = mm(PSf[:, (k % 2) * 1024 + t * P:(k % 2) * 1024 + (t + 1) * P],
                                  a[:, j, t * P:(t + 1) * P], w[:, k % 2, j],
                                  start=(j == 0 and n == 0), stop=(j == DJ - 1 and n == 2))
            return last

        def wait_chunk(s, raw, k):
            pe.wait_ge(raw_used, raw + k + 1)
            pe.wait_ge(evac_done, s + k + 1)

        def project(name, n):
            with pe.Fori(0, n // RAW) as i:
                for k in range(RAW):
                    wait_chunk(i * RAW + PROJ_AT[name], i * RAW + RAW_AT[name], k)
                    chunk_product(k).then_inc(proj_done, 1)

        pe.sem_inc(proj_done, 2)
        pe.sem_inc(gq_done, 2)
        pe.sem_inc(a_prod, 2)
        pe.sem_inc(v_prod, 16)
        pe.wait_ge(const_in, 16)
        pe.wait_ge(cs_done, 1)
        modulation("ada")
        variance(0)
        pe.wait_ge(hl_done, DJ)
        project("qkv", 8)
        for k in range(RAW):
            wait_chunk(PROJ_AT["qkv"] + 8, RAW_AT["qkv"] + 8, k)
            (chunk_product if k < 2 else chunk_product_tokens)(k).then_inc(proj_done, 1)

        for c in range(11):
            if c < 10:
                pe.wait_ge(hsq_done, c + 1)
                mm(PSf[:, (c % 2) * 1024:(c % 2) * 1024 + NS], HEADM, SQ[:, c % 2, 0:NS], start=True, stop=True)
                mm(PSf[:, (c % 2) * 1024 + NS:(c % 2) * 1024 + NT], HEADM, SQ[:, c % 2, NS:NT],
                   start=True, stop=True).then_inc(hvar_done, 1)
            if c > 0:
                pe.wait_ge(hq_done, c)
                if c > 2:
                    pe.wait_ge(hrope_done, c - 2)
                mm(PSf[:, 2048 + ((c - 1) % 2) * 512:2560 + ((c - 1) % 2) * 512], SWAP, BIG[:, c - 1, 0:NS],
                   start=True, stop=True).then_inc(hrot_done, 1)

        pe.wait_ge(hrope_done, 10)
        pe.wait_ge(cache_in, 32)
        for m in range(2):
            with pe.Fori(0, 4) as jj:
                j10 = jj * 10 + 40 * m
                pe.wait_ge(q_staged, jj + (4 * m + 1))

                def scores(u):
                    half, qt = u // 5, u % 5
                    a, b = half * HD, (half + 1) * HD
                    if u >= 2:
                        pe.wait_ge(exp_done, j10 + (u - 1))
                    q = QS[a:b, qt * P:(qt + 1) * P]
                    o = (u % 2) * 1024
                    if qt < 4:
                        mm(PSf[:, o:o + NS], q, BIG[a:b, 8 + m, 0:NS], start=True, stop=True)
                        last = mm(PSf[:, o + NS:o + NT], q, KC[a:b, m], start=True, stop=True)
                    else:
                        last = mm(PSf[:, o:o + NP], q, BIG[a:b, 8 + m, NS:NT], start=True, stop=True)
                    last.then_inc(score_done, 1)

                def turn(u):
                    pe.wait_ge(p_done, j10 + (u + 1))
                    if u >= 1:
                        pe.wait_ge(ptc_done, j10 + u)
                    for kt in range(5 if u % 5 < 4 else 1):
                        last = nc.tensor.transpose(PSf[:, 2048 + kt * P:2048 + (kt + 1) * P],
                                                   PR[:, u % 2, kt * P:(kt + 1) * P], ID)
                    last.then_inc(pt_done, 1)

                def values(u):
                    half, qt = u // 5, u % 5
                    pe.wait_ge(ptc_done, j10 + (u + 1))
                    if u == 0:
                        pe.wait_ge(oh_done, jj + (4 * m + 1))
                    out = PSf[half * HD:(half + 1) * HD, 3072 + qt * P:3072 + (qt + 1) * P]
                    n = 5 if qt < 4 else 1
                    for kt in range(n):
                        if qt == 4:
                            val = BIG[:, 10 + m, NS + half * HD:NS + (half + 1) * HD]
                        elif kt < 4:
                            val = BIG[:, 10 + m, kt * P + half * HD:kt * P + (half + 1) * HD]
                        else:
                            val = VC[:, m * P + half * HD:m * P + (half + 1) * HD]
                        last = mm(out, val, PT[:, u % 2, kt * P:(kt + 1) * P], start=(kt == 0), stop=(kt == n - 1))
                    last.then_inc(pv_done, 1)

                scores(0)
                scores(1)
                for u in range(11):
                    if u < 10:
                        turn(u)
                    if u + 2 < 10:
                        scores(u + 2)
                    if u >= 1:
                        values(u - 1)
        pe.wait_ge(act_lo, 1)
        project("wo", N_WO)

        def route_and_gather(l, name):
            variance(2 * l + 1)
            pe.wait_ge(hl_done, DJ * (2 * l + 2))
            project(name, N_PQ)
            pe.wait_ge(sk_in, 16 * (l + 1))
            pe.wait_ge(evac_done, 2 + PROJ_AT[name] + N_PQ)
            tiles = (TT - 1,) + tuple(range(TT - 1))

            def route_scores(r):
                t, n = tiles[r], l * TT + r
                if n > 0:
                    pe.wait_ge(route_read, n)
                for hc in range(HC):
                    last = mm(PSf[:, hc * P:(hc + 1) * P], BIG[:, hc, t * P:(t + 1) * P], SK[:, hc],
                              start=True, stop=True)
                last.then_inc(route_ps, 1)

            def picks(r):
                pe.wait_ge(pick_ready, l * 4 + r)
                pe.wait_ge(ht_done, l + 1)
                if r > 1:
                    pe.wait_ge(pick_done, l * 4 + r - 1)
                for q, src in enumerate((I12[:, 0], I12[:, 1], G[:].rearrange("p h k -> p (h k)"))):
                    last = nc.tensor.transpose(PSf[:, 2048 + q * P:2048 + (q + 1) * P], src, ID)
                last.then_inc(pick_ps, 1)

            def quads(tg):
                q0 = l * (NS // 4) + tg * (TG // 4)
                with pe.Fori(0, TG // 8) as i:
                    for par in range(2):
                        pe.wait_ge(oh_ready, i * 2 + (q0 + par + 1))
                        pe.wait_ge(gt_done, i * 2 + (q0 + par + 1))
                        for q in range(4):
                            last = mm(PSf[:, 3072 + par * 512 + q * P:3072 + par * 512 + (q + 1) * P],
                                      OH[:, par, q, 0], OH[:, par, q, 1], start=True, stop=True)
                        last.then_inc(gq_done, 1)

            route_scores(0)
            for j in range(DJ):
                last = nc.tensor.transpose(PSf[:, 2048 + j * P:2048 + (j + 1) * P], H[:, j, NS:NT], ID)
            last.then_inc(ht_ps, 1)
            if l == 0:
                modulation("ada1", 0, N_ADA // 2)
            route_scores(1)
            if l == 0:
                modulation("ada1", N_ADA // 2, N_ADA)
            route_scores(2)
            picks(1)
            for r in range(2, TT):
                quads(2 * (r - 2))
                if r + 1 < TT:
                    route_scores(r + 1)
                picks(r)
                quads(2 * (r - 2) + 1)
            quads(6)
            quads(7)
            pe.wait_ge(gt_done, 2 + (l + 1) * 128)

            r0 = RAW_AT[f"dense{l}"]

            def u_product(i, k, n):
                if isinstance(i, int) and i == 0 and k == 0:
                    pe.wait_ge(raw_used, r0 + 1)
                else:
                    pe.wait_ge(raw_used, i * 8 + (r0 + 2 * k))
                pe.wait_ge(gelu_done, n + 1)
                for j in range(DJ):
                    for q, (w, a) in enumerate(((SH, HH), (SH, HL), (SL, HH))):
                        last = mm(PSf[:, (k % 2) * 512:(k % 2) * 512 + NS], w[:, k % 2, j], a[:, j, 0:NS],
                                  start=(j == 0 and q == 0), stop=(j == DJ - 1 and q == 2))
                last.then_inc(a_prod, 1)

            def v_product(i, k, n):
                b0 = (k - 2 - k % 2) % 4
                if k % 2 == 0:
                    pe.wait_ge(wl_done, n + 2)
                    end = isinstance(i, int) and i == NB_E // 4
                    pe.wait_ge(raw_used, i * 8 + (r0 + 2 * k + (0 if end else 1)))
                for q in range(4):
                    dj = 4 * (k % 2) + q
                    pe.wait_ge(v_acc, (n - k % 2) * 4 + (dj - 8 + 1))
                    for b in range(2):
                        for m, (w, a) in enumerate(((VH, WH), (VH, WL), (VL, WH))):
                            last = mm(PSf[:, 1024 + q * 512:1536 + q * 512], w[:, b0 + b, dj], a[:, b0 + b],
                                      start=(b == 0 and m == 0), stop=(b == 1 and m == 2))
                    last.then_inc(v_prod, 1)

            def blocks(i, first=False):
                for k in range(4):
                    n = i * 4 + (l * NB_E + k)
                    u_product(i, k, n)
                    if not (first and k < 2):
                        v_product(i, k, n)

            blocks(0, first=True)
            with pe.Fori(1, NB_E // 4) as i:
                blocks(i)
            for k in range(2):
                v_product(NB_E // 4, k, (l + 1) * NB_E + k)
            pe.wait_ge(acc_done, l + 1)
            for j in range(DJ):
                last = nc.tensor.transpose(PSf[:, 3072 + j * P:3072 + (j + 1) * P], ACC[:, j * P:(j + 1) * P], ID)
            last.then_inc(yt_done, 1)

        route_and_gather(0, "pq")
        variance(2)
        pe.wait_ge(hl_done, 3 * DJ)
        project("bcx", N_BCX)
        pe.wait_ge(act_lo, 2)
        project("co", N_CO)
        route_and_gather(1, "pq1")
        variance(4)

    @block.scalar
    def _(act):
        def split_high(name, g, k, s):
            act.wait_ge(raw_in[k], g * 16 + 16)
            act.wait_ge(proj_done, s + 1)
            nc.scalar.copy(SH[:, k % 2], RW[:, k]).then_inc(hi_done, 1)

        def split_all(name, n):
            with act.Fori(0, n // RAW) as i:
                for k in range(RAW):
                    split_high(name, i + RAW_AT[name] // RAW, k, i * RAW + (PROJ_AT[name] + k))

        def norm(n):
            wait_x(act, n)
            for j in range(DJ):
                nc.scalar.square(H[:, j], X[:, j]).then_inc(sq_done, 1)
            act.wait_ge(var_done, n + 1)
            nc.scalar.activation(RR[:], PSf[:, 2048:2048 + NT], ACT.Sqrt, bias=EP[:]).then_inc(rt_done, 1)
            if n == 0:
                act.wait_ge(mod_done, 1)
            if n == 2:
                act.wait_ge(mod_done, 2)
            for j in range(DJ):
                act.wait_ge(xn_done, n * DJ + j + 1)
                if n == 4:
                    nc.scalar.activation(H[:, j], H[:, j], ACT.Copy, scale=GN[:, 4, j:j + 1]).then_inc(y_done, 1)
                    continue
                f = n % 2
                for s, (a, b) in enumerate(((NS, NT), (0, NS))):
                    nc.scalar.activation(H[:, j, a:b], H[:, j, a:b], ACT.Identity,
                                         scale=GS[:, n // 2, f, j, s:s + 1],
                                         bias=M[:, n // 2, 3 * f * DJ + j, s:s + 1])
                act.drain()
                nc.scalar.copy(HH[:, j], H[:, j]).then_inc(h_done, 1)

        act.wait_ge(eps_done, 1)
        act.wait_ge(small_in, 16 * 5)
        nc.scalar.activation(CS[:], CS[:], ACT.Silu).then_inc(cs_done, 1)
        act.dma_start(SK[:], subk[0]).then_inc(sk_in, 16)
        norm(0)
        act.wait_ge(hl_done, DJ)
        act.dma_start(KC[:], kcache).then_inc(cache_in, 16)
        act.dma_start(VC[:], vcache).then_inc(cache_in, 16)
        split_all("qkv", N_QKV)

        act.wait_ge(evac_done, 2 + N_QKV)
        act.dma_start(v_new, BIG[:, 10:12, NS:NT]).then_inc(out_done, 16)
        for c in range(11):
            if c < 10:
                if c >= 2:
                    act.wait_ge(hvar_done, c - 1)
                nc.scalar.square(SQ[:, c % 2], BIG[:, c]).then_inc(hsq_done, 1)
            if c >= 1:
                act.wait_ge(hvar_done, c)
                if c > 2:
                    act.wait_ge(hq_done, c - 2)
                nc.scalar.activation(RN[:, (c - 1) % 2], ps_pair((c - 1) % 2), ACT.Sqrt, bias=EP[:]).then_inc(hrt_done, 1)
        act.wait_ge(hrope_done, 10)
        act.dma_start(k_new, BIG[:, 8:10, NS:NT]).then_inc(out_done, 16)

        for m in range(2):
            with act.Fori(0, 4) as jj:
                j10 = jj * 10 + 40 * m
                nc.scalar.mul(QS[:], BIG[:, bass.ds(jj + 4 * m, 1)].rearrange("p o n -> p (o n)"), HD ** -0.5).then_inc(q_staged, 1)
                for u in range(11):
                    if u < 10:
                        w = NT if u % 5 < 4 else NP
                        act.wait_ge(nb_done, j10 + (u + 1))
                        nc.scalar.activation(PR[:, u % 2, 0:w], PSf[:, (u % 2) * 1024:(u % 2) * 1024 + w], ACT.Exp,
                                             bias=NB[:, u % 2:u % 2 + 1],
                                             accum_out=RS[:, u % 2:u % 2 + 1]).then_inc(exp_done, 1)
                    if u >= 1:
                        v = u - 1
                        w = NT if v % 5 < 4 else NP
                        act.wait_ge(pt_done, j10 + u)
                        if v >= 2:
                            act.wait_ge(pv_done, j10 + (v - 1))
                        nc.scalar.copy(PT[:, v % 2, 0:w], PSf[:, 2048:2048 + w]).then_inc(ptc_done, 1)
                act.wait_ge(pv_done, j10 + 10)
                nc.scalar.copy(HH[:, bass.ds(jj + 4 * m, 1)].rearrange("p o n -> p (o n)"),
                               PSf[:, 3072:3072 + NT]).then_inc(o_done, 1)
        split_all("wo", N_WO)

        def gathers(l, name):
            norm(2 * l + 1)
            split_all(name, N_PQ)
            def layout(tg):
                if tg > 0 or l > 0:
                    act.wait_ge(gw_done, 16 * (l * (NS // TG) + tg))
                with act.Fori(0, TG // 8) as i:
                    for par in range(2):
                        act.wait_ge(gq_done, i * 2 + ((l * 8 + tg) * (TG // 4) + par + 3))
                        out = GT[:, :, bass.ds(i * 8 + par * 4, 4)].rearrange("p i t -> p t i")
                        nc.scalar.copy(out, PSf[:, 3072 + par * 512:3072 + (par + 1) * 512].rearrange(
                            "p (t i) -> p t i", t=4)).then_inc(gt_done, 1)

            act.wait_ge(ht_ps, l + 1)
            nc.scalar.copy(HTOK[:], PSf[:, 2048:3072]).then_inc(ht_done, 1)
            for r in range(TT):
                if r > 1:
                    layout(2 * (r - 2))
                act.wait_ge(sm_in, l * TT + r + 1)
                nc.scalar.activation(G[:], G[:], ACT.Exp).then_inc(sm_out, 1)
                if r > 0:
                    act.wait_ge(pick_ps, l * 4 + r)
                    nc.scalar.copy(PK[:, r - 1].rearrange("p q t -> p (q t)"), PSf[:, 2048:2048 + 3 * P]).then_inc(pick_done, 1)
                if r > 1:
                    layout(2 * (r - 2) + 1)
            if l == 0:
                act.dma_start(SK[:], subk[1]).then_inc(sk_in, 16)
            layout(6)
            layout(7)

            g0 = RAW_AT[f"dense{l}"] // RAW

            def high(dst, i, r):
                act.wait_ge(raw_in[r % RAW], (i * 2 + (g0 + r // RAW + 1)) * 16)
                nc.scalar.copy(dst, RW[:, r % RAW]).then_inc(hi_done, 1)

            def blocks(i, last=False):
                for k in range(4):
                    n = i * 4 + (l * NB_E + k)
                    if not (last and k == 3):
                        act.wait_ge(a_prod, n + 2)
                        high(SH[:, (k + 1) % 2], i, 2 * k + 1)
                    act.wait_ge(v_prod, (n - k % 2) * 4 + 8)
                    high(VH[:, k], i, 2 * k + (1 if last and k == 3 else 2))
                    act.wait_ge(a_prod, n + 3)
                    act.wait_ge(wl_done, n + 1)
                    nc.scalar.activation(GE[:, k % 2], PSf[:, (k % 2) * 512:(k % 2) * 512 + NS],
                                         ACT.Gelu_apprx_tanh).then_inc(gelu_done, 1)
                    act.wait_ge(w_done, n + 5)
                    nc.scalar.copy(WH[:, k], GE[:, k % 2]).then_inc(wh_done, 1)

            act.wait_ge(a_prod, 2 + l * NB_E)
            high(SH[:, 0], 0, 0)
            with act.Fori(0, 16) as i:
                blocks(i)
            act.wait_ge(a_done, l + 1)
            nc.scalar.activation(AA[:], AA[:], ACT.Gelu_apprx_tanh).then_inc(g_done, 1)
            with act.Fori(16, 31) as i:
                blocks(i)
            blocks(31, last=True)

        gathers(0, "pq")
        norm(2)
        split_all("bcx", N_BCX)
        act.wait_ge(evac_done, 2 + PROJ_AT["co"])
        for j in range(DJ):
            last = nc.scalar.copy(HH[:, j], BIG[:, j])
        last.then_inc(act_hi, 1)
        split_all("co", N_CO)
        gathers(1, "pq1")
        norm(4)
        act.wait_ge(y_done, DJ)
        act.dma_start(yT, H[:]).then_inc(out_done, 16)
        act.wait_ge(out_done, 48)

    @block.vector
    def _(dve):
        v = nc.vector

        def modulation(l):
            name = "ada1" if l else "ada"
            dve.wait_ge(raw_used, RAW_AT[name] + N_ADA)
            v.tensor_tensor(M[:, l], PSf[:, 3072:3072 + 96].rearrange("p (c s) -> p c s", s=2),
                            BA[:, l].unsqueeze(2).to_broadcast([P, N_ADA, 2]), ALU.add)
            dve.drain()
            for f in range(2):
                last = v.scalar_tensor_tensor(GS[:, l, f], M[:, l, (3 * f + 1) * DJ:(3 * f + 2) * DJ], 1.0,
                                              GN[:, 2 * l + f].unsqueeze(2).to_broadcast([P, DJ, 2]), ALU.add, ALU.mult)
            last.then_inc(mod_done, 1)

        def norm(n):
            dve.wait_ge(rt_done, n + 1)
            v.reciprocal(RR[:], RR[:])
            dve.drain()
            for j in range(DJ):
                v.tensor_tensor(H[:, j], X[:, j], RR[:], ALU.mult).then_inc(xn_done, 1)
            if n == 4:
                return
            for j in range(DJ):
                dve.wait_ge(h_done, (n if n < 4 else 0) * DJ + j + 1)
                v.tensor_tensor(HL[:, j], H[:, j], HH[:, j].bitcast(F32), ALU.subtract).then_inc(hl_done, 1)

        def copy_out(name, n):
            with dve.Fori(0, n // RAW) as i:
                for k in range(RAW):
                    dve.wait_ge(proj_done, i * RAW + (PROJ_AT[name] + k + 3))
                    v.tensor_copy(BIG[:, bass.ds(i * RAW + k, 1)].rearrange("p o n -> p (o n)"),
                                  ps_pair(k % 2)).then_inc(evac_done, 1)

        def gate_scalar(i, k, l, s):
            return M[:, l].rearrange("p c s -> p (c s)")[:, bass.ds(i * (2 * RAW) + (2 * 2 * DJ + 2 * k + s), 1)]

        def residual_out(name, n):
            with dve.Fori(0, n // RAW) as i:
                for k in range(RAW):
                    dve.wait_ge(proj_done, i * RAW + (PROJ_AT[name] + k + 3))
                    for s, (a, b) in enumerate(((NS, NT), (0, NS))):
                        x = X[:, bass.ds(i * RAW + k, 1), a:b].rearrange("p o n -> p (o n)")
                        last = v.scalar_tensor_tensor(x, ps_pair(k % 2)[:, a:b], gate_scalar(i, k, int(name == "co"), s), x,
                                                      ALU.mult, ALU.add)
                    last.then_inc(evac_done, 1)

        def top16(vals, idx, src, wk, n, after_read=None):
            for i in range(n):
                v.max(vals[:, i, 0:8], src(i))
            dve.drain()
            for i in range(n):
                v.max_index(idx[:, i, 0:8], vals[:, i, 0:8], src(i))
                last = v.match_replace(wk(i), vals[:, i, 0:8], src(i), LOWEST)
            if after_read is not None:
                last.then_inc(after_read, 1)
            dve.drain()
            for i in range(n):
                v.max(vals[:, i, 8:16], wk(i))
            dve.drain()
            for i in range(n):
                v.max_index(idx[:, i, 8:16], vals[:, i, 8:16], wk(i))
            dve.drain()

        def route_halves(n):
            dve.wait_ge(route_ps, n + 1)
            top16(V16, I16, lambda i: PSf[:, i * P:(i + 1) * P], lambda i: WK[:, i], HC, route_read)
            v.tensor_copy(IF[:], I16[:])
            vv = V16[:].rearrange("p (h c) k -> p h c k", c=2)
            v.tensor_tensor(CAND[:], vv[:, :, 0].unsqueeze(3).to_broadcast([P, PH, TOPK, TOPK]),
                            vv[:, :, 1].unsqueeze(2).to_broadcast([P, PH, TOPK, TOPK]), ALU.add)
            dve.drain()

        def route(n, picks_before):
            cf = CAND[:].rearrange("p h a b -> p h (a b)")
            wf = WK[:].rearrange("p (h c) n -> p h (c n)", c=2)
            top16(TS, PO, lambda i: cf[:, i], lambda i: wf[:, i], PH)
            if picks_before:
                dve.wait_ge(pick_ps, picks_before)
            po = PO[:].rearrange("p h k -> p (h k)")
            v.tensor_scalar(AB[:, 0], po, 4, None, ALU.logical_shift_right)
            v.tensor_scalar(AB[:, 1], po, 15, None, ALU.bitwise_and)
            v.tensor_tensor(G[:], TS[:], TS[:, :, 0:1].to_broadcast([P, PH, TOPK]), ALU.subtract).then_inc(sm_in, 1)
            dve.drain()
            v.tensor_copy(ABF[:], AB[:])
            dve.drain()
            fi = IF[:].rearrange("p (h c) k -> p h c k", c=2)
            for c in range(2):
                v.tensor_tensor(EQ[:], ABF[:, c].unsqueeze(2).to_broadcast([P, PICKS, TOPK]),
                                J16.unsqueeze(1).to_broadcast([P, PICKS, TOPK]), ALU.is_equal)
                dve.drain()
                e4 = EQ[:].rearrange("p (h k) j -> p h k j", k=TOPK)
                v.tensor_tensor(e4, e4, fi[:, :, c].unsqueeze(2).to_broadcast([P, PH, TOPK, TOPK]), ALU.mult)
                dve.drain()
                v.tensor_reduce(I12[:, c], EQ[:], AX_X, ALU.add)
                dve.drain()
            if n % TT == 0:
                v.scalar_tensor_tensor(EI[:], I12[:, 0], float(NKEY), I12[:, 1], ALU.mult, ALU.add).then_inc(ei_done, 1)
            dve.wait_ge(sm_out, n + 1)
            v.tensor_reduce(Z[:], G[:], AX_X, ALU.add)
            dve.drain()
            v.reciprocal(Z[:], Z[:])
            dve.drain()
            v.tensor_tensor(G[:], G[:], Z[:].unsqueeze(2).to_broadcast([P, PH, TOPK]), ALU.mult)

        def experts(l):
            def one_hots(tg):
                tile, half = tg // 2, tg % 2
                dve.wait_ge(pick_done, l * 4 + tile + 1)
                pk = PK[:, tile]
                with dve.Fori(0, TG // 8) as i:
                    for par in range(2):
                        dve.wait_ge(gq_done, i * 2 + (l * 128 + tg * (TG // 4) + par + 1))
                        for q in range(4):
                            t = i * 8 + (half * TG + par * 4 + q)
                            v.tensor_scalar(OH[:, par, q, 0], IOTA, pk[:, 0, bass.ds(t, 1)], None, ALU.is_equal)
                            last = v.tensor_scalar(OH[:, par, q, 1], IOTA, pk[:, 1, bass.ds(t, 1)],
                                                   pk[:, 2, bass.ds(t, 1)], ALU.is_equal, ALU.mult)
                        last.then_inc(oh_ready, 1)

            for r in range(TT):
                route_halves(l * TT + r)
                if r > 1:
                    one_hots(2 * (r - 2))
                route(l * TT + r, l * 4 + max(r - 1, 0))
                if r == 0:
                    dve.drain()
                    v.tensor_copy(WW[:], G[:].rearrange("p h k -> p (h k)"))
                    dve.drain()
                else:
                    dve.drain().then_inc(pick_ready, 1)
                if l == 0 and r == 1:
                    modulation(1)
                if r > 1:
                    one_hots(2 * (r - 2) + 1)
            one_hots(6)
            one_hots(7)

            def wait_row(i, q):
                dve.wait_ge(row_in[q % RING], i * 32 + 16 * (l * 64 + q // RING + 1))

            def u_pick(i, q):
                wait_row(i, q)
                v.tensor_tensor_reduce(ROWS[:, q % RING], ROWS[:, q % RING], HTOK[:], 1.0, 0.0, ALU.mult, ALU.add,
                                       A16[:, q:q + 1]).then_inc(row_used, 1)

            def v_pick(i, q):
                wait_row(i, q)
                v.scalar_tensor_tensor(ACC[:], ROWS[:, q % RING], AA[:, bass.ds(i * 8 + (q - 128), 1)], ACC[:],
                                       ALU.mult, ALU.add).then_inc(row_used, 1)
                dve.drain()

            def add_chunk(n, k, q):
                dj = 4 * (k % 2) + q
                dve.wait_ge(v_prod, (n - k % 2) * 4 + (dj - 8 + 17))
                x = X[:, dj, 0:NS]
                v.scalar_tensor_tensor(x, PSf[:, 1024 + q * 512:1536 + q * 512], M[:, l, 5 * DJ + dj, 1:2], x,
                                       ALU.mult, ALU.add).then_inc(v_acc, 1)

            def blocks(i, pick, first=False):
                for k in range(4):
                    n = i * 4 + (l * NB_E + k)
                    dve.wait_ge(gelu_done, n + 3)
                    dve.wait_ge(gb_in[k], i * 16 + 16 * (l * 32 + 1))
                    v.tensor_tensor(GE[:, k % 2], GE[:, k % 2], GB[:, k], ALU.mult).then_inc(w_done, 1)
                    if not (first and k < 2):
                        add_chunk(n, k, 0)
                    dve.wait_ge(wh_done, n + 1)
                    v.tensor_tensor(WL[:, k], GE[:, k % 2], WH[:, k].bitcast(F32), ALU.subtract).then_inc(wl_done, 1)
                    for q in (2 * k, 2 * k + 1):
                        pick(i, q)
                    if not (first and k < 2):
                        for q in range(1, 4):
                            add_chunk(n, k, q)

            def u_blocks_(i, first=False):
                blocks(i, u_pick, first)
                dve.drain()
                v.tensor_copy(AA[:, bass.ds(i * 8, 8)], A16[:, 0:8])
                dve.drain()

            dve.wait_ge(ht_done, l + 1)
            blocks(0, u_pick, first=True)
            dve.drain()
            v.tensor_copy(AA[:, 0:8], A16[:, 0:8])
            dve.drain()
            with dve.Fori(1, 16) as i:
                u_blocks_(i)
            dve.drain().then_inc(a_done, 1)
            v.memset(ACC[:], 0.0)
            dve.wait_ge(g_done, l + 1)
            v.tensor_tensor(AA[:], AA[:], WW[:], ALU.mult)
            dve.drain()
            with dve.Fori(16, 32) as i:
                blocks(i, v_pick)
            dve.drain().then_inc(acc_done, 1)
            for k in range(2):
                for q in range(4):
                    add_chunk((l + 1) * NB_E + k, k, q)
            dve.wait_ge(yt_done, l + 1)
            for j in range(DJ):
                x = X[:, j, NS:NT]
                last = v.scalar_tensor_tensor(x, PSf[:, 3072 + j * P:3072 + (j + 1) * P],
                                              M[:, l, 5 * DJ + j, 0:1], x, ALU.mult, ALU.add)
            last.then_inc(peer_done, 1)

        dve.sem_inc(evac_done, 2)
        dve.sem_inc(row_used, RING)
        dve.sem_inc(gt_done, 2)
        dve.sem_inc(gelu_done, 2)
        dve.sem_inc(v_acc, 4)
        dve.sem_inc(wl_done, 2)
        dve.sem_inc(w_done, 4)
        dve.sem_inc(oh_done, 1)
        v.memset(EP[:], EPS).then_inc(eps_done, 1)
        dve.wait_ge(small_in, 16 * 5)
        modulation(0)
        norm(0)
        copy_out("qkv", N_QKV)
        for c in range(11):
            if c < 10:
                dve.wait_ge(hrt_done, c + 1)
                v.reciprocal(RN[:, c % 2], RN[:, c % 2])
                dve.drain()
                v.scalar_tensor_tensor(BIG[:, c], BIG[:, c], HG[:, c:c + 1], RN[:, c % 2],
                                       ALU.mult, ALU.mult).then_inc(hq_done, 1)
            if c >= 1:
                b = c - 1
                dve.wait_ge(hrot_done, c)
                v.tensor_tensor(TR[:, b % 2], PSf[:, 2048 + (b % 2) * 512:2560 + (b % 2) * 512], SIN, ALU.mult)
                v.tensor_tensor(BIG[:, b, 0:NS], BIG[:, b, 0:NS], COS, ALU.mult)
                dve.drain()
                v.tensor_tensor(BIG[:, b, 0:NS], BIG[:, b, 0:NS], TR[:, b % 2], ALU.add).then_inc(hrope_done, 1)

        for m in range(2):
            with dve.Fori(0, 4) as jj:
                j10 = jj * 10 + 40 * m
                for u in range(11):
                    if u < 10:
                        w = NT if u % 5 < 4 else NP
                        dve.wait_ge(score_done, j10 + (u + 1))
                        v.reduce_max(MX[:, u % 2:u % 2 + 1], PSf[:, (u % 2) * 1024:(u % 2) * 1024 + w], AX_X)
                        dve.drain()
                        v.tensor_scalar(NB[:, u % 2:u % 2 + 1], MX[:, u % 2:u % 2 + 1], -1.0, None,
                                        ALU.mult).then_inc(nb_done, 1)
                    if u >= 1:
                        b = u - 1
                        w = NT if b % 5 < 4 else NP
                        dve.wait_ge(exp_done, j10 + u)
                        v.reciprocal(RI[:, b % 2:b % 2 + 1], RS[:, b % 2:b % 2 + 1])
                        dve.drain()
                        v.tensor_scalar(PR[:, b % 2, 0:w], PR[:, b % 2, 0:w], RI[:, b % 2:b % 2 + 1], None,
                                        ALU.mult).then_inc(p_done, 1)
                dve.wait_ge(o_done, jj + (4 * m + 1))
                v.tensor_tensor(HL[:, bass.ds(jj + 4 * m, 1)].rearrange("p o n -> p (o n)"), PSf[:, 3072:3072 + NT],
                                HH[:, bass.ds(jj + 4 * m, 1)].rearrange("p o n -> p (o n)").bitcast(F32),
                                ALU.subtract).then_inc(oh_done, 1)
        dve.drain().then_inc(act_lo, 1)
        residual_out("wo", N_WO)
        norm(1)
        dve.wait_ge(out_done, 32)
        copy_out("pq", N_PQ)
        experts(0)
        norm(2)
        with dve.Fori(0, 2) as i:
            for q in range(12):
                jl, part = q // 3, q % 3
                dve.wait_ge(proj_done, i * 12 + (PROJ_AT["bcx"] + q + 3))
                ps = ps_pair(q % 2)
                cv = CV[:].rearrange("p j t -> p (j t)")

                def tap(n):
                    return cv[:, bass.ds(i * 16 + (jl * 4 + n), 1)]
                if part == 0:
                    v.tensor_copy(GC[:], ps).then_inc(evac_done, 1)
                    dve.drain()
                elif part == 1:
                    v.tensor_tensor(UU[:], GC[:], ps, ALU.mult).then_inc(evac_done, 1)
                    dve.drain()
                    v.tensor_scalar(CC[:], UU[:], tap(1), tap(3), ALU.mult, ALU.add)
                    dve.drain()
                    for a, b in ((0, NS), (NS, NT)):
                        v.scalar_tensor_tensor(CC[:, a + 1:b], UU[:, a:b - 1], tap(0), CC[:, a + 1:b], ALU.mult, ALU.add)
                    dve.drain()
                    for a, b in ((0, NS), (NS, NT)):
                        v.scalar_tensor_tensor(CC[:, a:b - 1], UU[:, a + 1:b], tap(2), CC[:, a:b - 1], ALU.mult, ALU.add)
                    dve.drain()
                else:
                    v.tensor_tensor(BIG[:, bass.ds(i * 4 + jl, 1)].rearrange("p o n -> p (o n)"), CC[:], ps,
                                    ALU.mult).then_inc(evac_done, 1)
                    dve.drain()
        dve.wait_ge(act_hi, 1)
        for j in range(DJ):
            last = v.tensor_tensor(HL[:, j], BIG[:, j], HH[:, j].bitcast(F32), ALU.subtract)
        last.then_inc(act_lo, 1)
        residual_out("co", N_CO)
        norm(3)
        copy_out("pq1", N_PQ)
        experts(1)
        norm(4)

    block_cm.__exit__(None, None, None)


def _constants():
    c = np.zeros((P, C_ALL), np.float32)
    p = np.arange(P)
    c[:, C_MEAN:C_MEAN + P] = 1.0 / D
    c[:, C_HEAD:C_HEAD + P] = (p[:, None] // HD == p[None, :] // HD) / np.float32(HD)
    c[:, C_SWAP:C_SWAP + P] = p[:, None] == (p[None, :] ^ 16)
    c[:, C_ID:C_ID + P] = np.eye(P)
    c[:, C_IOTA:C_IOTA + NKEY] = np.arange(NKEY)
    axis = HD // 2
    inv = (np.float32(10000.0) ** (-np.arange(0, axis, 2, dtype=np.float32) / np.float32(axis))).astype(np.float32)
    t = np.arange(NS)
    place = np.where((p % HD < axis)[:, None], (t // GRID_W)[None, :], (t % GRID_W)[None, :]).astype(np.float32)
    ang = (place * inv[p % 16][:, None]).astype(np.float32)
    c[:, C_COS:C_COS + NS] = np.cos(ang)
    c[:, C_SIN:C_SIN + NS] = np.sin(ang) * np.where(p % 32 < 16, -1.0, 1.0)[:, None]
    return c


def kernel(x_prompt, x_sample, cache_k, cache_v, c, c_ctx, w_ada, b_ada, norm_mix, norm_ffn, norm_final,
           w_qkv, q_gain, k_gain, w_o, w_bcx, conv_w, conv_b, w_conv_out, w_pq, sub_keys, u_exp, v_exp):
    import concourse.bacc as _bacc
    from concourse.bass_utils import run_bass_kernel_spmd as _run

    def cols(w):
        return np.ascontiguousarray(w.reshape(DJ, P, -1, P).transpose(2, 1, 0, 3))

    a = {k: np.asarray(v) for k, v in locals().items() if isinstance(v, (np.ndarray,)) or hasattr(v, "__array__")}
    heads = [(j // 4) * 8 + half * 4 + j % 4 for j in range(8) for half in range(2)]
    wqkv = a["w_qkv"][0]
    wq = wqkv[:, :HEADS * HD].reshape(D, HEADS, HD)[:, heads].reshape(D, D)
    wo = a["w_o"][0].reshape(HEADS, HD, D)[heads].reshape(D, D)
    bcx = cols(a["w_bcx"][0]).reshape(3, DJ, P, DJ, P)
    bcx = bcx[[1, 2, 0]].transpose(1, 0, 2, 3, 4).reshape(N_BCX, P, DJ, P)
    stream = np.concatenate([
        cols(a["w_ada"][0]), cols(wq), cols(wqkv[:, HEADS * HD:]), cols(wo), cols(a["w_pq"][0]),
        cols(a["w_ada"][1]), bcx, cols(a["w_conv_out"][0]), cols(a["w_pq"][1])])
    x = np.concatenate([a["x_sample"][0], a["x_prompt"][0]])
    by_chunk = lambda m: np.ascontiguousarray(m.reshape(m.shape[:-1] + (DJ, P)))
    ins = {
        "xT": np.ascontiguousarray(x.reshape(NT, DJ, P).transpose(2, 1, 0)),
        "cond": np.ascontiguousarray(np.stack([a["c_ctx"], a["c"][0]]).reshape(2, DJ, P).transpose(2, 1, 0)),
        "consts": _constants(),
        "wstream": stream,
        "bada": np.ascontiguousarray(a["b_ada"].reshape(DEPTH, N_ADA, P).transpose(2, 0, 1)),
        "gains": np.ascontiguousarray(by_chunk(np.stack([a["norm_mix"][0], a["norm_ffn"][0], a["norm_mix"][1],
                                                         a["norm_ffn"][1], a["norm_final"]])).transpose(2, 0, 1)),
        "hgain": np.ascontiguousarray(np.stack([np.concatenate([g, g]) for g in
                                                [a["q_gain"][0]] * 8 + [a["k_gain"][0]] * 2]).T),
        "convp": np.ascontiguousarray(by_chunk(np.concatenate([a["conv_w"][0], a["conv_b"]])).transpose(2, 1, 0)),
        "kcache": np.ascontiguousarray(a["cache_k"][0, 0].reshape(P, 2, P).transpose(2, 1, 0)),
        "vcache": np.ascontiguousarray(a["cache_v"][0, 0].reshape(P, 2 * P)),
        "subk": np.ascontiguousarray(a["sub_keys"].reshape(DEPTH, HC, NKEY, P).transpose(0, 3, 1, 2)),
        "u_blk": np.ascontiguousarray(a["u_exp"].reshape(DEPTH, NKEY, NB_E, DJ, P).transpose(0, 2, 4, 3, 1)),
        "v_blk": np.ascontiguousarray(a["v_exp"].reshape(DEPTH, NKEY, NB_E, DJ, P).transpose(0, 2, 1, 3, 4)),
        "u_exp0": a["u_exp"][0], "u_exp1": a["u_exp"][1], "v_exp0": a["v_exp"][0], "v_exp1": a["v_exp"][1],
    }
    outs = {"yT": (P, DJ, NT), "k_new": (P, 2, NP), "v_new": (P, 2, NP)}
    nc = _bacc.Bacc("TRN2", target_bir_lowering=False, num_devices=1)
    ap = {n: nc.dram_tensor(n, v.shape, F32, kind="ExternalInput").ap() for n, v in ins.items()}
    op = {n: nc.dram_tensor(n, s, F32, kind="ExternalOutput").ap() for n, s in outs.items()}
    hybrid_step(nc, ap["xT"], ap["cond"], ap["consts"], ap["wstream"], ap["bada"], ap["gains"], ap["hgain"],
                ap["convp"], ap["kcache"], ap["vcache"], ap["subk"], [ap["u_exp0"], ap["u_exp1"]],
                [ap["v_exp0"], ap["v_exp1"]], ap["u_blk"], ap["v_blk"],
                nc.dram_tensor("router_weights", (NB_E, P, NS), F32, kind="Internal").ap(), op["yT"], op["k_new"], op["v_new"])
    r = _run(nc, [ins], core_ids=[0]).results[0]
    y = r["yT"].transpose(2, 1, 0).reshape(NT, D)
    k = r["k_new"].transpose(2, 1, 0).reshape(1, 1, NP, KVH, HD)
    v = r["v_new"].reshape(1, 1, NP, KVH, HD)
    return (np.ascontiguousarray(y[NS:])[None], np.ascontiguousarray(y[:NS])[None],
            np.ascontiguousarray(k), np.ascontiguousarray(v))
```
